# Optimizing a Trainium2 kernel written in Bass

```python
import jax, jax.numpy as jnp
from jax import lax
import numpy as np

D_MODEL = 1024
BATCH = 1
SEQ = 256
DEPTH = 2

MOBA_HEADS = 8
HEAD_DIM = D_MODEL // MOBA_HEADS
ROT_DIM = HEAD_DIM // 4
ROPE_THETA = 500000.0
MOBA_BLOCK = 256
MOBA_TOPK = 3
MOBA_Q_CHUNK = 32
DSA_HEADS = 8
DSA_KV_HEADS = 2
DSA_TOPK_MAX = 256
DSA_Q_CHUNK = 128
IDX_HEADS = 8
IDX_DIM = 64
IDX_ROT_DIM = IDX_DIM // 4
D_FF = -(-8 * D_MODEL // (3 * 256)) * 256
MOBA_W = MOBA_HEADS * HEAD_DIM
DSA_QW = DSA_HEADS * HEAD_DIM
DSA_KVW = DSA_KV_HEADS * HEAD_DIM
IDX_QW = IDX_HEADS * IDX_DIM
IN_SIZES = (MOBA_W, MOBA_W, MOBA_W, DSA_QW, DSA_KVW, DSA_KVW, IDX_QW, IDX_DIM, IDX_HEADS, D_MODEL, D_MODEL)
N_IN = 3 * MOBA_W + DSA_QW + 2 * DSA_KVW + IDX_QW + IDX_DIM + IDX_HEADS + 2 * D_MODEL
N_MOD = 6
NORM_EPS = 1e-6
NEG_INF = -1e30

kernel_name = "hybrid_moba_dsa_gated_block"

def _rmsnorm(x, g):
    xf = x.astype(jnp.float32)
    y = xf * lax.rsqrt(jnp.mean(xf * xf, axis=-1, keepdims=True) + NORM_EPS)
    return (y * g.astype(jnp.float32)).astype(x.dtype)

def _partial_rope(x, pos, rot_dim):
    half = rot_dim // 2
    inv_freq = ROPE_THETA ** (-jnp.arange(half, dtype=jnp.float32) * 2.0 / rot_dim)
    ang = pos.astype(jnp.float32)[..., None] * inv_freq
    cos = jnp.cos(ang)[:, :, None, :]
    sin = jnp.sin(ang)[:, :, None, :]
    xf = x.astype(jnp.float32)
    x1 = xf[..., :half]
    x2 = xf[..., half:rot_dim]
    out = jnp.concatenate([x1 * cos - x2 * sin, x2 * cos + x1 * sin, xf[..., rot_dim:]], axis=-1)
    return out.astype(x.dtype)

def _moba_attention(q, k, v):
    bsz, seq, nh, dh = q.shape
    nb = -(-seq // MOBA_BLOCK)
    n_sel = min(MOBA_TOPK, nb)
    pad = nb * MOBA_BLOCK - seq
    kp = jnp.pad(k, ((0, 0), (0, pad), (0, 0), (0, 0)))
    vp = jnp.pad(v, ((0, 0), (0, pad), (0, 0), (0, 0)))
    kbh = kp.reshape(bsz, nb, MOBA_BLOCK, nh, dh).transpose(0, 3, 1, 2, 4)
    vbh = vp.reshape(bsz, nb, MOBA_BLOCK, nh, dh).transpose(0, 3, 1, 2, 4)
    kmean = jnp.mean(kbh.astype(jnp.float32), axis=3)
    n_chunks = seq // MOBA_Q_CHUNK
    qc = q.reshape(bsz, n_chunks, MOBA_Q_CHUNK, nh, dh).swapaxes(0, 1)
    bi = jnp.arange(bsz)[:, None, None, None]
    hi = jnp.arange(nh)[None, None, :, None]
    blk_ids = jnp.arange(nb)
    scale = dh ** -0.5

    def one_chunk(args):
        ci, qb = args
        start = ci * MOBA_Q_CHUNK
        q_pos = start + jnp.arange(MOBA_Q_CHUNK)
        own = start // MOBA_BLOCK
        gate = jnp.einsum('bqhd,bhnd->bqhn', qb.astype(jnp.float32), kmean)
        gate = jnp.where(blk_ids < own, gate, NEG_INF)
        _, sel = lax.top_k(gate, n_sel)
        sel_ok = sel < own
        k_sel = kbh[bi, hi, sel]
        v_sel = vbh[bi, hi, sel]
        k_own = lax.dynamic_slice_in_dim(kp, own * MOBA_BLOCK, MOBA_BLOCK, axis=1)
        v_own = lax.dynamic_slice_in_dim(vp, own * MOBA_BLOCK, MOBA_BLOCK, axis=1)
        own_pos = own * MOBA_BLOCK + jnp.arange(MOBA_BLOCK)
        causal = own_pos[None, :] <= q_pos[:, None]
        s_sel = jnp.einsum('bqhd,bqhjkd->bqhjk', qb, k_sel).astype(jnp.float32) * scale
        s_sel = jnp.where(sel_ok[..., None], s_sel, NEG_INF)
        s_sel = s_sel.reshape(bsz, MOBA_Q_CHUNK, nh, n_sel * MOBA_BLOCK)
        s_own = jnp.einsum('bqhd,bkhd->bqhk', qb, k_own).astype(jnp.float32) * scale
        s_own = jnp.where(causal[None, :, None, :], s_own, NEG_INF)
        p = jax.nn.softmax(jnp.concatenate([s_sel, s_own], axis=-1), axis=-1).astype(v.dtype)
        p_sel = p[..., :n_sel * MOBA_BLOCK].reshape(bsz, MOBA_Q_CHUNK, nh, n_sel, MOBA_BLOCK)
        p_own = p[..., n_sel * MOBA_BLOCK:]
        return (jnp.einsum('bqhjk,bqhjkd->bqhd', p_sel, v_sel)
                + jnp.einsum('bqhk,bkhd->bqhd', p_own, v_own))

    out = lax.map(one_chunk, (jnp.arange(n_chunks), qc))
    return out.swapaxes(0, 1).reshape(bsz, seq, nh * dh)

def _dsa_attention(q, k, v, qi, ki, wi):
    bsz, seq, nq, dh = q.shape
    nkv = k.shape[2]
    grp = nq // nkv
    n_top = min(DSA_TOPK_MAX, seq // 4)
    n_chunks = seq // DSA_Q_CHUNK
    qc = q.reshape(bsz, n_chunks, DSA_Q_CHUNK, nq, dh).swapaxes(0, 1)
    qic = qi.reshape(bsz, n_chunks, DSA_Q_CHUNK, IDX_HEADS, IDX_DIM).swapaxes(0, 1)
    wic = wi.reshape(bsz, n_chunks, DSA_Q_CHUNK, IDX_HEADS).swapaxes(0, 1)
    kif = ki.astype(jnp.float32)
    key_pos = jnp.arange(seq)
    bi = jnp.arange(bsz)[:, None, None]
    scale = dh ** -0.5
    idx_scale = IDX_DIM ** -0.5

    def one_chunk(args):
        ci, qb, qib, wib = args
        q_pos = ci * DSA_Q_CHUNK + jnp.arange(DSA_Q_CHUNK)
        logits = jnp.einsum('bqhd,bsd->bqhs', qib.astype(jnp.float32), kif) * idx_scale
        score = jnp.einsum('bqh,bqhs->bqs', wib.astype(jnp.float32), jax.nn.relu(logits))
        score = jnp.where(key_pos[None, None, :] <= q_pos[None, :, None], score, NEG_INF)
        _, idx = lax.top_k(score, n_top)
        valid = idx <= q_pos[None, :, None]
        k_sel = k[bi, idx]
        v_sel = v[bi, idx]
        qg = qb.reshape(bsz, DSA_Q_CHUNK, nkv, grp, dh)
        s = jnp.einsum('bqgrd,bqkgd->bqgrk', qg, k_sel).astype(jnp.float32) * scale
        s = jnp.where(valid[:, :, None, None, :], s, NEG_INF)
        p = jax.nn.softmax(s, axis=-1).astype(v.dtype)
        o = jnp.einsum('bqgrk,bqkgd->bqgrd', p, v_sel)
        return o.reshape(bsz, DSA_Q_CHUNK, nq, dh)

    out = lax.map(one_chunk, (jnp.arange(n_chunks), qc, qic, wic))
    return out.swapaxes(0, 1).reshape(bsz, seq, nq * dh)

def _layer(x, c, positions, w_ada, b_ada, g_pre_mix, g_post_mix, w_in, w_out,
           g_pre_ffn, g_post_ffn, w_gate, w_up, w_down):
    bsz, seq, _ = x.shape
    mod = jax.nn.silu(c) @ w_ada + b_ada
    sh1, sc1, gt1, sh2, sc2, gt2 = [m[:, None, :] for m in jnp.split(mod, N_MOD, axis=-1)]

    h = _rmsnorm(x, g_pre_mix) * (1.0 + sc1) + sh1
    proj = h @ w_in
    cuts = [int(v) for v in np.cumsum(IN_SIZES)[:-1]]
    (qa, ka, va, qb, kb, vb, qi, ki, wi, ga, gb) = jnp.split(proj, cuts, axis=-1)
    qa = _partial_rope(qa.reshape(bsz, seq, MOBA_HEADS, HEAD_DIM), positions, ROT_DIM)
    ka = _partial_rope(ka.reshape(bsz, seq, MOBA_HEADS, HEAD_DIM), positions, ROT_DIM)
    va = va.reshape(bsz, seq, MOBA_HEADS, HEAD_DIM)
    qb = _partial_rope(qb.reshape(bsz, seq, DSA_HEADS, HEAD_DIM), positions, ROT_DIM)
    kb = _partial_rope(kb.reshape(bsz, seq, DSA_KV_HEADS, HEAD_DIM), positions, ROT_DIM)
    vb = vb.reshape(bsz, seq, DSA_KV_HEADS, HEAD_DIM)
    qi = _partial_rope(qi.reshape(bsz, seq, IDX_HEADS, IDX_DIM), positions, IDX_ROT_DIM)
    ki = _partial_rope(ki[:, :, None, :], positions, IDX_ROT_DIM)[:, :, 0, :]
    wi = wi * (IDX_HEADS ** -0.5)
    y_a = _moba_attention(qa, ka, va)
    y_b = _dsa_attention(qb, kb, vb, qi, ki, wi)
    mixed = jax.nn.sigmoid(ga) * y_a + jax.nn.sigmoid(gb) * y_b
    x = x + gt1 * _rmsnorm(mixed @ w_out, g_post_mix)

    h = _rmsnorm(x, g_pre_ffn) * (1.0 + sc2) + sh2
    f = (jax.nn.silu(h @ w_gate) * (h @ w_up)) @ w_down
    return x + gt2 * _rmsnorm(f, g_post_ffn)

def setup_inputs(seed: int = 0) -> dict:
    key = jax.random.key(seed)
    ks = jax.random.split(key, 16)
    f32 = jnp.float32
    x = jax.random.normal(ks[0], (BATCH, SEQ, D_MODEL), f32)
    c = jax.random.normal(ks[1], (BATCH, D_MODEL), f32)
    offset = jax.random.randint(ks[2], (BATCH, 1), 0, 4096, dtype=jnp.int32)
    positions = (offset + jnp.arange(SEQ, dtype=jnp.int32)[None, :]).astype(jnp.int32)
    def nrm(k, shape, fan_in):
        return jax.random.normal(k, shape, f32) * (fan_in ** -0.5)
    def gain(k):
        return 1.0 + 0.05 * jax.random.normal(k, (DEPTH, D_MODEL), f32)
    return {
        "x": x,
        "c": c,
        "positions": positions,
        "w_ada": nrm(ks[3], (DEPTH, D_MODEL, N_MOD * D_MODEL), D_MODEL),
        "b_ada": 0.01 * jax.random.normal(ks[4], (DEPTH, N_MOD * D_MODEL), f32),
        "g_pre_mix": gain(ks[5]),
        "g_post_mix": gain(ks[6]),
        "w_in": nrm(ks[7], (DEPTH, D_MODEL, N_IN), D_MODEL),
        "w_out": nrm(ks[8], (DEPTH, D_MODEL, D_MODEL), D_MODEL),
        "g_pre_ffn": gain(ks[9]),
        "g_post_ffn": gain(ks[10]),
        "w_gate": nrm(ks[11], (DEPTH, D_MODEL, D_FF), D_MODEL),
        "w_up": nrm(ks[12], (DEPTH, D_MODEL, D_FF), D_MODEL),
        "w_down": nrm(ks[13], (DEPTH, D_FF, D_MODEL), D_FF),
    }

def reference(x, c, positions, w_ada, b_ada, g_pre_mix, g_post_mix, w_in, w_out,
              g_pre_ffn, g_post_ffn, w_gate, w_up, w_down):
    for l in range(DEPTH):
        x = _layer(x, c, positions, w_ada[l], b_ada[l], g_pre_mix[l], g_post_mix[l],
                   w_in[l], w_out[l], g_pre_ffn[l], g_post_ffn[l],
                   w_gate[l], w_up[l], w_down[l])
    return x


_drawn_inputs = setup_inputs


def setup_inputs(seed=0):
    import zlib

    import numpy as np

    out = dict(_drawn_inputs(seed))
    spreads = {}
    factors = {}
    for name, (base, spread) in spreads.items():
        noise = np.random.default_rng([zlib.crc32(name.encode()), seed]).standard_normal(out[name].shape)
        drawn = base * np.exp(spread * noise) if base else spread * noise
        out[name] = __import__('jax').numpy.asarray(drawn.astype(out[name].dtype))
    for name, factor in factors.items():
        out[name] = (out[name] * factor).astype(out[name].dtype)
    return out
```

```python
from contextlib import ExitStack

import numpy as np

import concourse.bass as bass
from concourse import mybir

P = 128
D = 1024
SEQ = 256
DEPTH = 2
TT = SEQ // P
KT = D // P
DH = 128
HALF = DH // 4 // 2
IH, IDH = 8, 64
IHALF = IDH // 4 // 2
FF = 2816
N_TOP = SEQ // 4
THETA = 500000.0
EPS = 1e-6
NEG = -1e30
TAKEN = -3e38
SCALE = DH ** -0.5
KV_HEADS = 2

UNIT = 2048
SMALL = IDH + IH
N_CHUNK = 15
MOBA0, DSA0 = 3, 11
N_FF = FF // 256
OUT_UNIT = 1 + 2 * (N_CHUNK - 1)
FFN_UNIT = OUT_UNIT + KT // 2
UNITS = FFN_UNIT + 3 * N_FF
RAW, RING = 3, 5
PIECE = 1024
PARTS = 6
ADA_RING = 2
N_CONST = P + 3 * P + HALF

F32 = mybir.dt.float32
F32R = mybir.dt.float32r
I32 = mybir.dt.int32
ALU = mybir.AluOpType
ACT = mybir.ActivationFunctionType

SH1, SC1, GT1, SH2, SC2, GT2 = range(6)


def up_unit(j):
    return FFN_UNIT + (3 * j - 1 if j else 0)


def down_unit(j):
    return FFN_UNIT + (3 * j + 4 if j < N_FF - 1 else 3 * j + 2)


def chunk_units(c):
    return [0] if c == 0 else [2 * c - 1, 2 * c]


def two_pi_parts():
    rest, parts = 2 * np.pi, []
    for low in (9, 21, 33, 45):
        part = np.floor(rest * 2.0 ** low) / 2.0 ** low
        parts.append(float(part))
        rest -= part
    return parts


RSQRT_BITS = 1597463007.0
NEWTON = 3
ROUND = 1.5 * 2.0 ** 23
PI_IN = 3.1415925

SPLITS = {2: [u + RING for u in (0, 1, 2)]} | {s: [u + RING for u in chunk_units(s - 1)] for s in range(3, N_CHUNK + 1)} \
    | {N_CHUNK + 1: [OUT_UNIT + RING], N_CHUNK + 2: [OUT_UNIT + 1 + RING, OUT_UNIT + 2 + RING]}


def ffn_part(l, j):
    at = {1: (l, GT2, 0), 2: (l, GT2, 4), 4: (l + 1, SC1, 0), 5: (l + 1, SC1, 4), 7: (l + 1, SH1, 0), 8: (l + 1, SH1, 4)}.get(j)
    if at is None or at[0] == DEPTH:
        return None
    return at[0], at[1], range(at[2], at[2] + 4)


HEADS = 16


def hybrid_decoder_trunk(nc, x_in, c_in, pos_in, const_in, w_ada, b_ada, gains, w_stream, out):
    with ExitStack() as ctx:
        def sb(name, shape, dt=F32):
            return ctx.enter_context(nc.sbuf_tensor(name, shape, dt))

        def sem(name):
            return ctx.enter_context(nc.semaphore(name))

        ps = ctx.enter_context(nc.psum_tensor("ps", [P, 8, 512], F32))
        QKT, SCO, PTB, OUT = 4, 5, 6, 7

        raw = sb("raw", [P, RAW, UNIT])
        w_hi = sb("w_hi", [P, RING, UNIT], F32R)
        w_lo = sb("w_lo", [P, RING, UNIT], F32R)
        ada = sb("ada", [P, ADA_RING, PIECE])

        x = sb("x", [P, TT, D])
        t_hi = sb("t_hi", [P, KT, SEQ], F32R)
        t_lo = sb("t_lo", [P, KT, SEQ], F32R)
        mixed = sb("mixed", [P, TT, D])
        scale_t = sb("scale_t", [P, D])
        shift_t = sb("shift_t", [P, D])
        gate_t = sb("gate_t", [P, D])
        acc = sb("acc", [P, D])

        pj = sb("pj", [P, 3, TT, 512])
        hbuf = pj[:, :, :, :].rearrange("p b t n -> p b (t n)")
        junk = hbuf[:, 2, :]
        kiw = sb("kiw", [P, TT, SMALL])
        kid = sb("kid", [P, TT, 2, IDH])
        kiT = sb("kiT", [P, SEQ])
        region = sb("region", [P, 4 * SEQ])
        qiT = region[:, :].rearrange("p (b n) -> p b n", b=4)
        sx = region[:, 0:3 * P]
        prob = region[:, 3 * P:6 * P]
        qkT = sb("qkT", [P, 512])
        kbT = sb("kbT", [P, 512])
        vb = sb("vb", [P, TT, 256])
        relu = sb("relu", [P, 2, 3 * P])
        probT = relu[:, 0, :]
        ffn_s = relu[:, :, 0:256]
        score = sb("score", [P, 3 * P])
        keep = sb("keep", [P, 3 * P])
        ffn_m = sb("ffn_m", [P, TT, 256])
        m_hi = sb("m_hi", [P, 2, 2, SEQ], F32R)
        m_lo = sb("m_lo", [P, 2, 2, SEQ], F32R)
        rope_a, rope_b = ffn_m[:, 0, :], ffn_m[:, 1, :]

        const = sb("const", [P, N_CONST])
        ident = const[:, 0:P]
        causal = const[:, P:4 * P]
        inv_freq = const[:, 4 * P:4 * P + HALF]
        ones = sb("ones", [P, P])
        pos = sb("pos", [P, TT], I32)
        cT = sb("cT", [P, KT])
        cs = sb("cs", [P, KT])
        posf = sb("posf", [P, TT])
        ang = sb("ang", [P, 6, TT, HALF])
        cos_t = sb("cos_t", [P, TT, 2 * HALF])
        sin_t = sb("sin_t", [P, TT, 2 * HALF])
        icos_t = sb("icos_t", [P, TT, 2 * IHALF])
        isin_t = sb("isin_t", [P, TT, 2 * IHALF])
        wis = sb("wis", [P, TT, IH])
        gtmp = kiT[:, :].rearrange("p (t n) -> p t n", t=TT)
        max8 = sb("max8", [P, 2, 8])
        ssq = sb("ssq", [P, TT])
        rstd = sb("rstd", [P, TT])
        rms = sb("rms", [P, TT, 2])
        nmax = sb("nmax", [P, 2, TT])
        rsum = sb("rsum", [P, 2, TT])
        rinv = sb("rinv", [P, TT])

        s_c = sem("c_landed")
        s_const = sem("const_landed")
        s_x = sem("x_landed")
        s_raw = [sem(f"raw_landed{i}") for i in range(RAW)]
        s_ada = [sem(f"ada_landed{i}") for i in range(ADA_RING)]
        s_bias = sem("bias_landed")
        s_bias1 = sem("bias1_landed")
        s_gscale = sem("scale_gain_landed")
        s_ggate = sem("gate_gain_landed")
        s_out = sem("out_stored")
        s_zero = sem("acc_zeroed")
        s_cs = sem("silu_c")
        s_sin = sem("sines")
        s_hi = sem("hi_split")
        s_pj = sem("pj_copied")
        s_iqk = sem("index_qk_copied")
        s_qkT = sem("qkT_copied")
        s_relu = sem("logits_rectified")
        s_exp = sem("exp_done")
        s_pT = sem("probT_copied")
        s_act_hi = sem("act_hi_split")
        s_sq = sem("squares_summed")
        s_silu = sem("silu_done")
        s_lo = sem("lo_split")
        s_roped = sem("roped")
        s_ang = sem("angles")
        s_iacc = sem("index_summed")
        s_ttr = sem("masked_min")
        s_gated = sem("head_gated")
        s_act_lo = sem("act_lo_split")
        s_h = sem("h_ready")
        s_xup = sem("x_updated")
        s_m = sem("m_ready")
        s_adause = sem("ada_used")
        s_table = sem("table_made")
        s_dve = sem("dve_chain")
        s_ones = sem("ones_set")
        s_rstd = sem("rstd_ready")
        s_mm = sem("projected")
        s_used = sem("unit_used")
        s_iT = sem("index_turned")
        s_qT = sem("qk_turned")
        s_logit = sem("index_logits")
        s_sco = sem("scores")
        s_prT = sem("prob_turned")
        s_av = sem("head_out")
        s_turn = sem("act_turned")
        s_y = sem("sublayer_out")
        s_up = sem("up_projected")
        s_adasum = sem("modulation_summed")

        N_MM, N_ROPE, N_QT, N_TURN = 2 * N_CHUNK, N_CHUNK, N_CHUNK - 2, 12 + 2 * N_FF
        PRO_SUM = 4

        def mm_no(c, t):
            return 2 * t + c + 1 if c < 2 else 2 * c + t + 1

        def turn_no(kind, i):
            return {"h1": 0, "mix": 4, "h2": 8, "m": 12}[kind] + i + 1

        def vhead(c, b=0):
            return c - MOBA0 if c < DSA0 else 8 + 2 * (c - DSA0) + b

        def is_head(c):
            return MOBA0 <= c < N_CHUNK

        def is_pair(c):
            return DSA0 <= c < N_CHUNK

        used_units = ([chunk_units(c)[0] for c in range(1, N_CHUNK)] + [OUT_UNIT + i for i in range(KT // 2 - 1)]
                      + sorted([up_unit(j) for j in range(N_FF)] + [down_unit(j) for j in range(N_FF - 1)]))
        N_USED = len(used_units)

        def wait_multiplied(eng, U):
            l, u = U // UNITS, U % UNITS
            if u in used_units:
                eng.wait_ge(s_used, l * N_USED + used_units.index(u) + 1)
            elif u < OUT_UNIT:
                eng.wait_ge(s_mm, l * N_MM + mm_no(u // 2, 1))
            elif u == FFN_UNIT - 1:
                eng.wait_ge(s_y, 4 * l + 2)
            elif u == UNITS - 1:
                eng.wait_ge(s_y, 4 * l + 4)
            else:
                j = [up_unit(j) + 1 for j in range(N_FF)].index(u)
                eng.wait_ge(s_up, 2 * (l * N_FF + j) + 2)

        block = ctx.enter_context(nc.Block())

        @block.sync
        def _(sp):
            pieces = [0]

            def load_unit(l, u):
                U = l * UNITS + u
                if U >= DEPTH * UNITS:
                    return
                if U >= RAW:
                    sp.wait_ge(s_lo, U - RAW + 1)
                n = KT * SMALL if U % UNITS == 0 else UNIT
                sp.dma_start(raw[:, U % RAW, 0:n], w_stream[U // UNITS, U % UNITS, :, 0:n]).then_inc(s_raw[U % RAW], 16)

            def load_pieces(l, part, ks):
                for k in ks:
                    n = pieces[0]
                    if n >= ADA_RING:
                        sp.wait_ge(s_adause, n - ADA_RING + 1)
                    sp.dma_start(ada[:, n % ADA_RING, :],
                                 w_ada[l, k * P:(k + 1) * P, part * D:(part + 1) * D]).then_inc(s_ada[n % ADA_RING], 16)
                    pieces[0] += 1

            sp.dma_start(cT[:], c_in).then_inc(s_c, 16)
            sp.dma_start(const[:], const_in).then_inc(s_const, 16)
            sp.dma_start(pos[:], pos_in).then_inc(s_const, 16)
            load_pieces(0, SC1, range(KT // 2))
            sp.dma_start(x[:, :, :], x_in).then_inc(s_x, 16)
            load_pieces(0, SC1, range(KT // 2, KT))
            load_pieces(0, SH1, range(KT))
            for u in range(RING):
                load_unit(0, u)
            for l in range(DEPTH):
                load_pieces(l, GT1, (0, 1))
                for s in range(2, N_CHUNK + 1):
                    split = SPLITS[s]
                    for half in range(2):
                        for u in split[:-1] if half == 0 else split[-1:]:
                            load_unit(l, u)
                        if s <= 12:
                            load_pieces(l, (GT1, SC2, SH2)[(s - 1) // 4], [2 * ((s - 1) % 4) + half])
                for u in range(OUT_UNIT + RING, OUT_UNIT + RING + 3):
                    load_unit(l, u)
                for j in range(N_FF):
                    if j != 1:
                        load_unit(l, up_unit(j) - 1 + RING if j == 0 else down_unit(j - 2) + RING)
                    ada_part = ffn_part(l, j)
                    if ada_part:
                        load_pieces(*ada_part[0:2], ada_part[2][:2])
                    for u in (up_unit(j), up_unit(j) + 1):
                        load_unit(l, u + RING)
                    if ada_part:
                        load_pieces(*ada_part[0:2], ada_part[2][2:])
                for u in (UNITS - 2, UNITS - 1):
                    load_unit(l, u + RING)
            for t in range(TT):
                sp.wait_ge(s_xup, 4 * (DEPTH - 1) + 3 + t)
                sp.dma_start(out[t], x[:, t, :]).then_inc(s_out, 16)
            sp.wait_ge(s_out, 16 * TT)

        @block.gpsimd
        def _(pool):
            def seed(buf, n, l, part, summed):
                if summed:
                    pool.wait_ge(s_adasum, summed)
                nc.gpsimd.memset(buf[:, :], 0.0).then_inc(s_zero, 1)
                pool.wait_ge(s_zero, n + 1)
                pool.dma_start(buf[0:1, :], b_ada[l:l + 1, part * D:(part + 1) * D]).then_inc(s_bias1 if n == 1 else s_bias, 16)

            def gain(table, l, which, landed):
                pool.dma_start(table[:, :], gains[which, l:l + 1, :].broadcast_to([P, D])).then_inc(landed, 16)

            seed(acc, 0, 0, SC1, 0)
            seed(gate_t, 1, 0, SH1, 0)
            gain(scale_t, 0, 0, s_gscale)
            for l in range(DEPTH):
                n = 2 + l * PARTS
                seed(acc, n, l, GT1, 2 * n if l else 2)
                if l:
                    pool.wait_ge(s_xup, 4 * l)
                else:
                    pool.wait_ge(s_adasum, PRO_SUM)
                gain(gate_t, l, 1, s_ggate)
                seed(acc, n + 1, l, SC2, 2 * n + 2)
                pool.wait_ge(s_h, 4 * l + 2)
                gain(scale_t, l, 2, s_gscale)
                seed(acc, n + 2, l, SH2, 2 * n + 4)
                seed(acc, n + 3, l, GT2, 2 * n + 6)
                pool.wait_ge(s_xup, 4 * l + 2)
                gain(gate_t, l, 3, s_ggate)
                if l + 1 < DEPTH:
                    seed(acc, n + 4, l + 1, SC1, 2 * n + 8)
                    pool.wait_ge(s_h, 4 * l + 4)
                    gain(scale_t, l + 1, 0, s_gscale)
                    seed(acc, n + 5, l + 1, SH1, 2 * n + 10)

        @block.scalar
        def _(act):
            def split_hi(l, u):
                U = l * UNITS + u
                if U >= DEPTH * UNITS:
                    return
                n = KT * SMALL if U % UNITS == 0 else UNIT
                act.wait_ge(s_raw[U % RAW], 16 * (U // RAW + 1))
                if U >= RING:
                    wait_multiplied(act, U - RING)
                nc.scalar.activation(w_hi[:, U % RING, 0:n], raw[:, U % RAW, 0:n], ACT.Copy).then_inc(s_hi, 1)

            def copy_chunk(l, c, t):
                act.wait_ge(s_mm, l * N_MM + mm_no(c, t))
                src = ps[:, (c % 2) + 2 * t, :]
                if c == 0:
                    nc.scalar.activation(kiw[:, t, :], src[:, 0:SMALL], ACT.Copy).then_inc(s_pj, 1)
                    return
                dst = pj[:, c % 3, t, :]
                if c == 1:
                    act.wait_ge(s_turn, l * N_TURN + turn_no("h1", 3))
                elif c == 4:
                    act.wait_ge(s_iT, l * 3 + 3)
                elif c == 5:
                    act.wait_ge(s_qT, l * N_QT + 1)
                elif c > 5:
                    act.wait_ge(s_gated, l * HEADS + vhead(c - 3, 1 if is_pair(c - 3) else 0) + 1)
                if c == 1:
                    nc.scalar.activation(dst, src, ACT.Copy).then_inc(s_pj, 1)
                elif c == 2:
                    nc.scalar.activation(dst[:, 0:256], src[:, 0:256], ACT.Copy)
                    nc.scalar.activation(vb[:, t, :], src[:, 256:512], ACT.Copy).then_inc(s_pj, 1)
                elif not is_pair(c):
                    nc.scalar.activation(dst[:, 0:384], src[:, 0:384], ACT.Copy)
                    nc.scalar.activation(dst[:, 384:512], src[:, 384:512], ACT.Tanh, scale=0.5).then_inc(s_pj, 1)
                else:
                    d = dst.rearrange("p (h a n) -> p h a n", h=2, a=2)
                    q = src.rearrange("p (h a n) -> p h a n", h=2, a=2)
                    nc.scalar.activation(d[:, :, 0, :], q[:, :, 0, :], ACT.Copy)
                    nc.scalar.activation(d[:, :, 1, :], q[:, :, 1, :], ACT.Tanh, scale=0.5).then_inc(s_pj, 1)

            def softmax_exp(l, v):
                n = l * HEADS + v
                act.wait_ge(s_ttr, n + 1)
                if n:
                    act.wait_ge(s_prT, n)
                if n > 1:
                    act.wait_ge(s_gated, n - 1)
                nc.scalar.activation(prob[:, 0:P], sx[:, 0:P], ACT.Exp, bias=nmax[:, v % 2, 0:1], scale=-1.0,
                                     accum_out=rsum[:, v % 2, 0:1])
                nc.scalar.activation(prob[:, P:3 * P], sx[:, P:3 * P], ACT.Exp, bias=nmax[:, v % 2, 1:2], scale=-1.0,
                                     accum_out=rsum[:, v % 2, 1:2]).then_inc(s_exp, 1)

            def copy_probT(l, v):
                act.wait_ge(s_prT, l * HEADS + v + 1)
                if v:
                    act.wait_ge(s_av, l * HEADS + v)
                else:
                    act.wait_ge(s_iacc, 4 * l + 4)
                nc.scalar.activation(probT, ps[:, PTB, 0:3 * P], ACT.Copy).then_inc(s_pT, 1)

            def copy_qkT(l, c):
                act.wait_ge(s_qT, l * N_QT + c - 1)
                if c == 2:
                    nc.scalar.activation(kbT[:, :], ps[:, QKT, :], ACT.Copy).then_inc(s_qkT, 1)
                    return
                if c > MOBA0:
                    act.wait_ge(s_sco, l * HEADS + vhead(c - 1, 1 if is_pair(c - 1) else 0) + 1)
                nc.scalar.activation(qkT[:, :], ps[:, QKT, :], ACT.Copy).then_inc(s_qkT, 1)

            def copy_index(l):
                act.wait_ge(s_iT, l * 3 + 1)
                nc.scalar.activation(kiT[:, :], ps[:, OUT, 0:SEQ], ACT.Copy).then_inc(s_iqk, 1)
                for i, bank in enumerate((QKT, PTB)):
                    act.wait_ge(s_iT, l * 3 + 2 + i)
                    nc.scalar.activation(region[:, 512 * i:512 * i + 512], ps[:, bank, :], ACT.Copy).then_inc(s_iqk, 1)

            def rectify(l, i):
                act.wait_ge(s_logit, 4 * l + i + 1)
                if i:
                    act.wait_ge(s_iacc, 4 * l + i)
                for b, bank in enumerate((SCO, OUT)):
                    ins = nc.scalar.activation(relu[:, b, :], ps[:, bank, 0:3 * P], ACT.Relu, scale=float(IDH) ** -0.5)
                ins.then_inc(s_relu, 1)

            def act_hi(l, kind, i, dst, src):
                act.wait_ge(s_turn, l * N_TURN + turn_no(kind, i))
                nc.scalar.activation(dst, src, ACT.Copy).then_inc(s_act_hi, 1)

            def h_hi(l, kind, t):
                for i in range(2):
                    act_hi(l, kind, 2 * t + i, t_hi[:, 4 * i:4 * i + 4, t * P:(t + 1) * P],
                           ps[:, PTB + i, :].rearrange("p (k n) -> p k n", k=4))

            def mix_hi(l, i):
                act_hi(l, "mix", i, t_hi[:, 2 * i:2 * i + 2, :],
                       ps[:, 3 if i == 0 else QKT, :].rearrange("p (k n) -> p k n", k=2))

            def m_hi_split(l, j, t):
                act_hi(l, "m", 2 * j + t, m_hi[:, j % 2, :, t * P:(t + 1) * P],
                       ps[:, PTB + t, 0:256].rearrange("p (k n) -> p k n", k=2))

            def sum_squares(n, t, src):
                if n >= 2:
                    act.wait_ge(s_rstd, n - 1)
                if n:
                    act.wait_ge(s_sq, n)
                nc.scalar.activation(junk, src, ACT.Square, scale=float(D) ** -0.5,
                                     accum_out=ssq[:, t:t + 1]).then_inc(s_sq, 1)

            def border(l, mid):
                n = 2 + 8 * l + (0 if mid else 4)
                for t in range(TT):
                    act.wait_ge(s_y, 4 * l + (0 if mid else 2) + t + 1)
                    sum_squares(n + t, t, ps[:, 2 * t:2 * t + 2, :].rearrange("p b n -> p (b n)"))
                if not mid and l + 1 == DEPTH:
                    return
                for t in range(TT):
                    act.wait_ge(s_xup, 4 * l + (0 if mid else 2) + t + 1)
                    sum_squares(n + 2 + t, t, x[:, t, :])

            act.wait_ge(s_c, 16)
            nc.scalar.activation(cs[:, :], cT[:, :], ACT.Silu).then_inc(s_cs, 1)
            act.wait_ge(s_ang, 1)
            nc.scalar.activation(ang[:, 4:6], ang[:, 2:4], ACT.Sin).then_inc(s_sin, 1)
            act.wait_ge(s_x, 16)
            for t in range(TT):
                sum_squares(t, t, x[:, t, :])
            for u in range(RAW):
                split_hi(0, u)

            for l in range(DEPTH):
                h_hi(l, "h1", 0)
                if l:
                    split_hi(l, RING - 1)
                copy_chunk(l, 0, 0)
                h_hi(l, "h1", 1)
                if l == 0:
                    for u in range(RAW, RING):
                        split_hi(0, u)
                copy_chunk(l, 1, 0)
                for s in range(2, N_CHUNK + 3):
                    if s == 2:
                        copy_chunk(l, 0, 1)
                    if s - 1 < N_CHUNK:
                        copy_chunk(l, s - 1, 1)
                    if is_head(s - 2):
                        softmax_exp(l, vhead(s - 2))
                    if s in (3, 4):
                        rectify(l, 2 * (s - 3))
                    if is_pair(s - 3):
                        copy_probT(l, vhead(s - 3, 1))
                    if s > N_CHUNK:
                        mix_hi(l, s - N_CHUNK)
                    for u in SPLITS[s][:-1]:
                        split_hi(l, u)
                    if s == 2:
                        copy_index(l)
                    elif s - 1 < N_CHUNK:
                        copy_qkT(l, s - 1)
                    if is_head(s - 2):
                        copy_probT(l, vhead(s - 2))
                    if is_pair(s - 2):
                        softmax_exp(l, vhead(s - 2, 1))
                    if s in (3, 4):
                        rectify(l, 2 * (s - 3) + 1)
                    if s < N_CHUNK:
                        copy_chunk(l, s, 0)
                    if s == N_CHUNK:
                        mix_hi(l, 0)
                    if s == N_CHUNK + 2:
                        mix_hi(l, 3)
                    split_hi(l, SPLITS[s][-1])

                border(l, True)
                for t in range(TT):
                    h_hi(l, "h2", t)
                for j in range(N_FF):
                    if j:
                        m_hi_split(l, j - 1, 1)
                    if j != 1:
                        split_hi(l, up_unit(j) - 1 + RING if j == 0 else down_unit(j - 2) + RING)
                    for t in range(TT):
                        act.wait_ge(s_up, 2 * (l * N_FF + j) + t + 1)
                        n = l * N_FF + j
                        if n:
                            act.wait_ge(s_m, 2 * n + t - 1)
                        nc.scalar.activation(ffn_s[:, t, :], ps[:, QKT + t, 0:256], ACT.Silu).then_inc(s_silu, 1)
                    m_hi_split(l, j, 0)
                    for u in (up_unit(j), up_unit(j) + 1):
                        split_hi(l, u + RING)
                m_hi_split(l, N_FF - 1, 1)
                split_hi(l, UNITS - 2 + RING)
                border(l, False)

        @block.vector
        def _(dve):
            links = [0]

            def link(ins):
                ins.then_inc(s_dve, 1)
                links[0] += 1
                dve.wait_ge(s_dve, links[0])

            def split_lo(l, u):
                U = l * UNITS + u
                if U >= DEPTH * UNITS:
                    return
                n = KT * SMALL if U % UNITS == 0 else UNIT
                dve.wait_ge(s_hi, U + 1)
                nc.vector.tensor_tensor(w_lo[:, U % RING, 0:n], raw[:, U % RAW, 0:n],
                                        w_hi[:, U % RING, 0:n].bitcast(F32), ALU.subtract).then_inc(s_lo, 1)

            pieces = [0]

            def add_pieces(count, buf):
                for _ in range(count):
                    n = pieces[0]
                    k = n % KT
                    if k == 0:
                        part = n // KT
                        dve.wait_ge(s_bias1 if part == 1 else s_bias, 16 * max(part, 1))
                    dve.wait_ge(s_ada[n % ADA_RING], 16 * (n // ADA_RING + 1))
                    if n:
                        dve.wait_ge(s_adause, n)
                    nc.vector.scalar_tensor_tensor(out=buf[:, :], in0=ada[:, n % ADA_RING, :], scalar=cs[:, k:k + 1],
                                                   in1=buf[:, :], op0=ALU.mult, op1=ALU.add).then_inc(s_adause, 1)
                    pieces[0] += 1

            def make_table(n, half, bank, kind, gain_count):
                cols = slice(512 * half, 512 * half + 512)
                dve.wait_ge(s_adasum, 2 * n + half + 1)
                if kind == "scale":
                    dve.wait_ge(s_gscale, 16 * gain_count)
                    ins = nc.vector.scalar_tensor_tensor(out=scale_t[:, cols], in0=ps[:, bank, :], scalar=1.0,
                                                         in1=scale_t[:, cols], op0=ALU.add, op1=ALU.mult)
                elif kind == "shift":
                    ins = nc.vector.tensor_copy(shift_t[:, cols], ps[:, bank, :])
                else:
                    dve.wait_ge(s_ggate, 16 * gain_count)
                    ins = nc.vector.tensor_tensor(gate_t[:, cols], ps[:, bank, :], gate_t[:, cols], ALU.mult)
                ins.then_inc(s_table, 1)

            def rotate(src, dst, heads, width, cos, sin, done):
                half = width // 2
                a = rope_a[:, 0:TT * heads * width].rearrange("p (t h w) -> p t h w", t=TT, h=heads)
                b = rope_b[:, 0:TT * heads * width].rearrange("p (t h w) -> p t h w", t=TT, h=heads)
                for t in range(TT):
                    cb = cos[:, t:t + 1, :].broadcast_to([P, heads, width])
                    sn = sin[:, t:t + 1, :].broadcast_to([P, heads, width])
                    nc.vector.tensor_tensor(a[:, t], src[:, t], cb, ALU.mult)
                    ins = nc.vector.tensor_tensor(b[:, t], src[:, t], sn, ALU.mult)
                link(ins)
                for t in range(TT):
                    x1, x2 = dst[t]
                    h = x1.shape[1]
                    a1 = a[:, t] if h == heads else a[:, t].broadcast_to([P, h, width])
                    b1 = b[:, t] if h == heads else b[:, t].broadcast_to([P, h, width])
                    nc.vector.tensor_tensor(x1, a1[:, :, 0:half], b1[:, :, half:], ALU.add)
                    ins = nc.vector.tensor_tensor(x2, a1[:, :, half:], b1[:, :, 0:half], ALU.add)
                ins.then_inc(s_roped, 1)
                dve.wait_ge(s_roped, done)

            def rope(l, c):
                done = l * N_ROPE + c + 1
                dve.wait_ge(s_pj, l * N_MM + (3 if c == 0 else 2 * c + 2))
                if c == 0:
                    nc.vector.tensor_scalar(wis[:, :, :], kiw[:, :, IDH:], float(IH) ** -0.5, None, ALU.mult)
                    nc.vector.tensor_copy(kid[:, :, 0, :], kiw[:, :, 0:IDH])
                    link(nc.vector.tensor_copy(kid[:, :, 1, :], kiw[:, :, 0:IDH]))
                    src = kiw[:, :, 0:2 * IHALF].rearrange("p t (h w) -> p t h w", h=1)
                    dst = [(kid[:, t, :, 0:IHALF], kid[:, t, :, IHALF:2 * IHALF]) for t in range(TT)]
                    rotate(src, dst, 1, 2 * IHALF, icos_t, isin_t, done)
                    return
                b = pj[:, c % 3, :, :]
                if c == 1:
                    v = b.rearrange("p t (h w) -> p t h w", h=IH)
                    rotate(v[:, :, :, 0:2 * IHALF],
                           [(v[:, t, :, 0:IHALF], v[:, t, :, IHALF:2 * IHALF]) for t in range(TT)],
                           IH, 2 * IHALF, icos_t, isin_t, done)
                    return
                v = b.rearrange("p t (h w) -> p t h w", h=2 if is_pair(c) else 4)[:, :, 0:2, :]
                rotate(v[:, :, :, 0:2 * HALF],
                       [(v[:, t, :, 0:HALF], v[:, t, :, HALF:2 * HALF]) for t in range(TT)],
                       2, 2 * HALF, cos_t, sin_t, done)

            def mask_scores(l, v):
                n = l * HEADS + v
                dve.wait_ge(s_sco, n + 1)
                if n:
                    dve.wait_ge(s_exp, n)
                m = causal if v < 8 else keep
                for t, cols in enumerate((slice(0, P), slice(P, 3 * P))):
                    ins = nc.vector.tensor_tensor_reduce(sx[:, cols], ps[:, SCO, cols], m[:, cols], -SCALE, 3e38,
                                                         ALU.add, ALU.min, nmax[:, v % 2, t:t + 1])
                ins.then_inc(s_ttr, 1)

            def gate_head(l, c, b):
                v = vhead(c, b)
                gates = pj[:, c % 3, :, (384 if v < 8 else 128 + 256 * b):][:, :, 0:P]
                dve.wait_ge(s_exp, l * HEADS + v + 1)
                nc.vector.reciprocal(rinv[:, :], rsum[:, v % 2, :])
                link(nc.vector.tensor_scalar(gates, gates, 0.5, 0.5, ALU.mult, ALU.add))
                dve.wait_ge(s_av, l * HEADS + v + 1)
                cols = slice((v % 8) * DH, (v % 8 + 1) * DH)
                for t in range(TT):
                    dst = mixed[:, t, cols] if v < 8 else gtmp[:, t, :]
                    ins = nc.vector.scalar_tensor_tensor(out=dst, in0=ps[:, OUT, t * P:(t + 1) * P],
                                                         scalar=rinv[:, t:t + 1], in1=gates[:, t, :],
                                                         op0=ALU.mult, op1=ALU.mult)
                if v >= 8:
                    link(ins)
                    ins = nc.vector.tensor_tensor(mixed[:, :, cols], mixed[:, :, cols], gtmp, ALU.add)
                ins.then_inc(s_gated, 1)
                dve.wait_ge(s_gated, l * HEADS + v + 1)

            def add_index(l, i):
                dve.wait_ge(s_relu, 4 * l + i + 1)
                for b in range(2):
                    for t, cols in enumerate((slice(0, P), slice(P, 3 * P))):
                        first = i == 0 and b == 0
                        ins = nc.vector.scalar_tensor_tensor(
                            out=score[:, cols], in0=relu[:, b, cols], scalar=wis[:, t, 2 * i + b:2 * i + b + 1],
                            in1=causal[:, cols] if first else score[:, cols], op0=ALU.mult, op1=ALU.add)
                    if b == 0:
                        link(ins)
                ins.then_inc(s_iacc, 1)
                dve.wait_ge(s_iacc, 4 * l + i + 1)

            def take_top(last):
                for t, cols in enumerate((slice(0, P), slice(P, 3 * P))):
                    ins = nc.vector.max(max8[:, t, :], score[:, cols])
                link(ins)
                for t, cols in enumerate((slice(0, P), slice(P, 3 * P))):
                    ins = nc.vector.match_replace(score[:, cols], max8[:, t, :], score[:, cols], TAKEN)
                link(ins)
                if last:
                    link(nc.vector.tensor_scalar(keep[:, :], score[:, :], 0.5 * TAKEN, NEG, ALU.is_gt, ALU.mult))
                    link(nc.vector.tensor_tensor(keep[:, :], keep[:, :], causal, ALU.add))

            def act_lo(l, kind, i, dst, src, hi):
                dve.wait_ge(s_act_hi, l * N_TURN + turn_no(kind, i))
                nc.vector.tensor_tensor(dst, src, hi.bitcast(F32), ALU.subtract).then_inc(s_act_lo, 1)

            def h_lo(l, kind, t):
                for i in range(2):
                    at = (slice(None), slice(4 * i, 4 * i + 4), slice(t * P, (t + 1) * P))
                    act_lo(l, kind, 2 * t + i, t_lo[at], ps[:, PTB + i, :].rearrange("p (k n) -> p k n", k=4), t_hi[at])

            def mix_lo(l, i):
                at = (slice(None), slice(2 * i, 2 * i + 2), slice(None))
                act_lo(l, "mix", i, t_lo[at], ps[:, 3 if i == 0 else QKT, :].rearrange("p (k n) -> p k n", k=2), t_hi[at])

            def m_lo_split(l, j, t):
                at = (slice(None), j % 2, slice(None), slice(t * P, (t + 1) * P))
                act_lo(l, "m", 2 * j + t, m_lo[at], ps[:, PTB + t, 0:256].rearrange("p (k n) -> p k n", k=2), m_hi[at])

            def inverse_rms(n, t):
                v, y, e = rms[:, t, 0:1], rstd[:, t:t + 1], rms[:, t, 1:2]
                dve.wait_ge(s_sq, n + 1)
                link(nc.vector.tensor_scalar(v, ssq[:, t:t + 1], EPS, None, ALU.add))
                link(nc.vector.tensor_scalar(y.bitcast(I32), v.bitcast(I32), -0.5, RSQRT_BITS, ALU.mult, ALU.add))
                for step in range(NEWTON):
                    link(nc.vector.scalar_tensor_tensor(out=e, in0=y, scalar=v, in1=y, op0=ALU.mult, op1=ALU.mult))
                    link(nc.vector.tensor_scalar(e, e, -0.5, 1.5, ALU.mult, ALU.add))
                    ins = nc.vector.tensor_tensor(y, y, e, ALU.mult)
                    if step < NEWTON - 1:
                        link(ins)
                ins.then_inc(s_rstd, 1)
                dve.wait_ge(s_rstd, n + 1)

            def norm_scale(n, t):
                inverse_rms(n, t)
                link(nc.vector.scalar_tensor_tensor(out=hbuf[:, t, :], in0=x[:, t, :], scalar=rstd[:, t:t + 1],
                                                    in1=scale_t[:, :], op0=ALU.mult, op1=ALU.mult))

            def norm_shift(t):
                nc.vector.tensor_tensor(hbuf[:, t, :], hbuf[:, t, :], shift_t[:, :], ALU.add).then_inc(s_h, 1)

            def pre_norm(l, kind, n, units=()):
                norm_scale(n, 0)
                norm_shift(0)
                norm_scale(n + 1, 1)
                h_lo(l, kind, 0)
                for u in units:
                    split_lo(l, u)
                norm_shift(1)
                h_lo(l, kind, 1)

            def add_sublayer(l, mid, n):
                for t in range(TT):
                    inverse_rms(n + t, t)
                    y = ps[:, 2 * t:2 * t + 2, :].rearrange("p b n -> p (b n)")
                    link(nc.vector.scalar_tensor_tensor(out=hbuf[:, t, :], in0=y, scalar=rstd[:, t:t + 1],
                                                        in1=gate_t[:, :], op0=ALU.mult, op1=ALU.mult))
                    nc.vector.tensor_tensor(x[:, t, :], x[:, t, :], hbuf[:, t, :], ALU.add).then_inc(s_xup, 1)
                    dve.wait_ge(s_xup, 4 * l + (0 if mid else 2) + t + 1)

            nc.vector.memset(ones[:, :], 1.0).then_inc(s_ones, 1)
            dve.wait_ge(s_const, 32)
            link(nc.vector.tensor_copy(posf[:, :], pos[:, :]))
            th, r, turns, high, low = ang[:, 0], ang[:, 2], ang[:, 1], ang[:, 4], ang[:, 5]
            for t in range(TT):
                ins = nc.vector.tensor_scalar(th[:, t, :], inv_freq, posf[:, t:t + 1], None, ALU.mult)
            link(ins)
            link(nc.vector.tensor_scalar(turns, th, 1.0 / (2 * np.pi), ROUND, ALU.mult, ALU.add))
            link(nc.vector.tensor_scalar(turns, turns, -ROUND, None, ALU.add))
            link(nc.vector.tensor_scalar(high, turns, ROUND * 2.0 ** 11, None, ALU.add))
            link(nc.vector.tensor_scalar(high, high, -ROUND * 2.0 ** 11, None, ALU.add))
            link(nc.vector.tensor_tensor(low, turns, high, ALU.subtract))
            parts = two_pi_parts()
            link(nc.vector.scalar_tensor_tensor(out=r, in0=high, scalar=-parts[0], in1=th, op0=ALU.mult, op1=ALU.add))
            for which, part in ((low, 0), (high, 1), (low, 1), (high, 2), (low, 2), (high, 3)):
                link(nc.vector.scalar_tensor_tensor(out=r, in0=which, scalar=-parts[part], in1=r,
                                                    op0=ALU.mult, op1=ALU.add))
            link(nc.vector.tensor_scalar(r, r, PI_IN, -PI_IN, ALU.min, ALU.max))
            quarter = ang[:, 3]
            link(nc.vector.tensor_scalar(quarter, r, np.pi / 2, None, ALU.add))
            link(nc.vector.tensor_scalar(turns, quarter, np.pi, -2 * np.pi, ALU.is_gt, ALU.mult))
            link(nc.vector.tensor_tensor(quarter, quarter, turns, ALU.add))
            nc.vector.tensor_scalar(quarter, quarter, PI_IN, -PI_IN, ALU.min, ALU.max).then_inc(s_ang, 1)
            dve.wait_ge(s_cs, 1)
            add_pieces(KT // 2, acc)
            dve.wait_ge(s_sin, 1)
            sine, cosine = ang[:, 4], ang[:, 5]
            for w, c_t, s_t, step in ((HALF, cos_t, sin_t, 1), (IHALF, icos_t, isin_t, HALF // IHALF)):
                for i in range(2):
                    nc.vector.tensor_copy(c_t[:, :, i * w:(i + 1) * w], cosine[:, :, ::step])
                nc.vector.tensor_copy(s_t[:, :, 0:w], sine[:, :, ::step])
                ins = nc.vector.tensor_scalar(s_t[:, :, w:], sine[:, :, ::step], -1.0, None, ALU.mult)
            link(ins)
            add_pieces(KT // 2, acc)
            add_pieces(KT, gate_t)
            for half in range(2):
                make_table(0, half, PTB + half, "scale", 1)
            for half in range(2):
                make_table(1, half, QKT + half, "shift", 0)
            dve.wait_ge(s_table, 4)
            pre_norm(0, "h1", 0, range(RAW))
            for u in range(RAW, RING):
                split_lo(0, u)

            for l in range(DEPTH):
                n_part = 2 + l * PARTS
                if l:
                    split_lo(l, RING - 1)
                add_pieces(2, acc)
                for s in range(2, N_CHUNK + 3):
                    if is_head(s - 2):
                        mask_scores(l, vhead(s - 2))
                    if s - 1 in (4, 8, 12):
                        i = (s - 5) // 4
                        for half in range(2):
                            make_table(n_part + i, half, (QKT, PTB)[half], ("gate", "scale", "shift")[i], 2 * l + (1, 2, 0)[i])
                    if s == 2:
                        rope(l, 0)
                    if s - 1 < N_CHUNK:
                        rope(l, s - 1)
                    if s in (3, 4):
                        add_index(l, 2 * (s - 3))
                    if is_head(s - 3):
                        gate_head(l, s - 3, 0)
                    if s > N_CHUNK:
                        mix_lo(l, s - N_CHUNK)
                    for u in SPLITS[s][:-1]:
                        split_lo(l, u)
                    if s <= 12:
                        add_pieces(1, acc)
                    if is_pair(s - 2):
                        mask_scores(l, vhead(s - 2, 1))
                    if is_pair(s - 3):
                        gate_head(l, s - 3, 1)
                    if s in (3, 4):
                        add_index(l, 2 * (s - 3) + 1)
                    if 5 <= s <= 12:
                        take_top(s == 12)
                    if s == N_CHUNK:
                        mix_lo(l, 0)
                    if s == N_CHUNK + 2:
                        mix_lo(l, 3)
                    split_lo(l, SPLITS[s][-1])
                    if s <= 12:
                        add_pieces(1, acc)

                add_sublayer(l, True, 2 + 8 * l)
                pre_norm(l, "h2", 4 + 8 * l)
                for j in range(N_FF):
                    part = ffn_part(l, j)
                    if j:
                        m_lo_split(l, j - 1, 1)
                    if j != 1:
                        split_lo(l, up_unit(j) - 1 + RING if j == 0 else down_unit(j - 2) + RING)
                    if part:
                        add_pieces(2, acc)
                    i = {3: 3, 6: 4, 9: 5}.get(j)
                    if i and (i == 3 or l + 1 < DEPTH):
                        kind, gains_so_far = {3: ("gate", 2 * l + 2), 4: ("scale", 2 * l + 3), 5: ("shift", 0)}[i]
                    else:
                        kind = None
                    for t in range(TT):
                        dve.wait_ge(s_silu, 2 * (l * N_FF + j) + t + 1)
                        if j:
                            dve.wait_ge(s_turn, l * N_TURN + turn_no("m", 2 * (j - 1) + t))
                        nc.vector.tensor_tensor(ffn_m[:, t, :], ffn_s[:, t, :], ps[:, QKT + t, 256:512],
                                                ALU.mult).then_inc(s_m, 1)
                        if kind:
                            make_table(n_part + i, t, PTB + t, kind, gains_so_far)
                        if t == 0 and not kind:
                            pass
                        if t == 0:
                            m_lo_split(l, j, 0)
                    for u in (up_unit(j), up_unit(j) + 1):
                        split_lo(l, u + RING)
                    if part:
                        add_pieces(2, acc)
                m_lo_split(l, N_FF - 1, 1)
                split_lo(l, UNITS - 2 + RING)
                add_sublayer(l, False, 6 + 8 * l)
                if l + 1 < DEPTH:
                    dve.wait_ge(s_table, 4 + 12 * (l + 1))
                    pre_norm(l + 1, "h1", 8 + 8 * l)

        @block.tensor
        def _(pe):
            def product(dst, hi, lo, w_h, w_l, first, last):
                nc.tensor.matmul(dst, hi, w_h, start=first, stop=False)
                nc.tensor.matmul(dst, hi, w_l, start=False, stop=False)
                return nc.tensor.matmul(dst, lo, w_h, start=False, stop=last)

            def project(l, c, t):
                units = chunk_units(c)
                cols = SMALL if c == 0 else 512
                bank = (c % 2) + 2 * t
                if c < 2:
                    if l:
                        pe.wait_ge(s_xup, 4 * l - 1 + t)
                    pe.wait_ge(s_act_lo, l * N_TURN + turn_no("h1", 2 * t + 1))
                elif c == 2:
                    pe.wait_ge(s_pj, l * N_MM + 1 + 2 * t)
                else:
                    pe.wait_ge(s_pj, l * N_MM + mm_no(c - 2, t))
                per = KT // len(units)
                for k in range(KT):
                    U = l * UNITS + units[k // per]
                    if t == 0 and k % per == 0:
                        pe.wait_ge(s_lo, U + 1)
                    a = (k % per) * cols
                    ins = product(ps[:, bank, 0:cols], t_hi[:, k, t * P:(t + 1) * P], t_lo[:, k, t * P:(t + 1) * P],
                                  w_hi[:, U % RING, a:a + cols], w_lo[:, U % RING, a:a + cols], k == 0, k == KT - 1)
                    if t == 1 and k == per - 1 < KT - 1:
                        ins.then_inc(s_used, 1)
                ins.then_inc(s_mm, 1)

            def down(l, u, hi, lo, first, last, signal):
                U = l * UNITS + u
                pe.wait_ge(s_lo, U + 1)
                for t in range(TT):
                    for n in range(2):
                        for k in range(2):
                            a = k * D + n * 512
                            ins = product(ps[:, 2 * t + n, :], hi[:, k, t * P:(t + 1) * P], lo[:, k, t * P:(t + 1) * P],
                                          w_hi[:, U % RING, a:a + 512], w_lo[:, U % RING, a:a + 512],
                                          first and k == 0, last and k == 1)
                    if signal:
                        ins.then_inc(s_y, 1)
                if not signal:
                    ins.then_inc(s_used, 1)

            def turn(dst, blocks, signal):
                for i, blk in enumerate(blocks):
                    ins = nc.tensor.transpose(dst[:, i * P:(i + 1) * P], blk, ident)
                ins.then_inc(signal, 1)

            def turn_h(l, kind, t, h_count):
                pe.wait_ge(s_h, h_count)
                for i in range(2):
                    if t:
                        pe.wait_ge(s_act_lo, l * N_TURN + turn_no(kind, i))
                    turn(ps[:, PTB + i, :], [hbuf[:, t, (4 * i + k) * P:(4 * i + k + 1) * P] for k in range(4)], s_turn)

            def turn_index(l):
                pe.wait_ge(s_roped, l * N_ROPE + 2)
                turn(ps[:, OUT, :], [kid[:, t, :, :].rearrange("p a n -> p (a n)") for t in range(TT)], s_iT)
                for i, bank in enumerate((QKT, PTB)):
                    turn(ps[:, bank, :], [pj[:, 1, t, (2 * i + j) * P:(2 * i + j + 1) * P]
                                          for j in range(2) for t in range(TT)], s_iT)

            def turn_qk(l, c):
                pe.wait_ge(s_roped, l * N_ROPE + c + 1)
                if c == 2:
                    pe.wait_ge(s_iqk, 3 * l + 2)
                else:
                    pe.wait_ge(s_qkT, l * N_QT + c - 2)
                if c - MOBA0 in (2, 6, 10):
                    pe.wait_ge(s_table, 4 + 12 * l + 2 * ((c - MOBA0 - 2) // 4) + 1)
                step = 2 if is_pair(c) else 1
                turn(ps[:, QKT, :], [pj[:, c % 3, t, step * j * P:(step * j + 1) * P]
                                     for j in range(2) for t in range(TT)], s_qT)

            def index_logits(l, i):
                pe.wait_ge(s_iqk, 3 * l + 3)
                if i:
                    pe.wait_ge(s_relu, 4 * l + i)
                for b, bank in enumerate((SCO, OUT)):
                    rows = slice(IDH * b, IDH * (b + 1))
                    for t in range(TT):
                        ins = nc.tensor.matmul(ps[:, bank, t * P:(2 * t + 1) * P],
                                               qiT[rows, i, t * P:(t + 1) * P], kiT[rows, 0:(t + 1) * P],
                                               start=True, stop=True)
                ins.then_inc(s_logit, 1)

            def scores(l, c, b):
                v = vhead(c, b)
                n = l * HEADS + v
                pe.wait_ge(s_qkT, l * N_QT + c - 1)
                if v == 0:
                    pe.wait_ge(s_relu, 4 * l + 4)
                else:
                    pe.wait_ge(s_ttr, n)
                q = qkT[:, 256 * b:256 * b + SEQ]
                kv = (v - 8) // (8 // KV_HEADS)
                k = qkT[:, SEQ:] if v < 8 else kbT[:, kv * SEQ:(kv + 1) * SEQ]
                nc.tensor.matmul(ps[:, SCO, 0:P], q[:, 0:P], k[:, 0:P], start=True, stop=True)
                nc.tensor.matmul(ps[:, SCO, P:3 * P], q[:, P:SEQ], k, start=True, stop=True).then_inc(s_sco, 1)

            def turn_prob(l, v):
                n = l * HEADS + v
                pe.wait_ge(s_exp, n + 1)
                if v:
                    pe.wait_ge(s_pT, n)
                else:
                    pe.wait_ge(s_iqk, 3 * l + 3)
                if v in (2, 6):
                    pe.wait_ge(s_table, 4 + 12 * l + 2 * ((v - 2) // 4) + 2)
                if v == 9:
                    pe.wait_ge(s_table, 4 + 12 * l + 6)
                turn(ps[:, PTB, :], [prob[:, i * P:(i + 1) * P] for i in range(3)], s_prT)

            def weigh_values(l, c, b):
                v = vhead(c, b)
                n = l * HEADS + v
                pe.wait_ge(s_pT, n + 1)
                if n:
                    pe.wait_ge(s_gated, n)
                if v < 8:
                    val = pj[:, c % 3, :, 256:384]
                else:
                    kv = (v - 8) // (8 // KV_HEADS)
                    val = vb[:, :, kv * DH:(kv + 1) * DH]
                nc.tensor.matmul(ps[:, OUT, 0:P], probT[:, 0:P], val[:, 0, :], start=True, stop=True)
                nc.tensor.matmul(ps[:, OUT, P:2 * P], probT[:, P:2 * P], val[:, 0, :], start=True, stop=False)
                nc.tensor.matmul(ps[:, OUT, P:2 * P], probT[:, 2 * P:3 * P], val[:, 1, :],
                                 start=False, stop=True).then_inc(s_av, 1)

            def sum_modulation(n, half, bank, buf):
                pe.wait_ge(s_adause, KT * (n + 1))
                nc.tensor.matmul(ps[:, bank, :], ones[:, :], buf[:, 512 * half:512 * half + 512],
                                 start=True, stop=True).then_inc(s_adasum, 1)

            def turn_mixed(l, i):
                pe.wait_ge(s_gated, l * HEADS + 8 + 2 * i + 2)
                if i == 0:
                    pe.wait_ge(s_pj, l * N_MM + 2 * (N_CHUNK - 2) + 2)
                else:
                    pe.wait_ge(s_qkT, l * N_QT + N_QT)
                    if i > 1:
                        pe.wait_ge(s_act_lo, l * N_TURN + turn_no("mix", i - 1))
                turn(ps[:, 3 if i == 0 else QKT, :],
                     [mixed[:, t, (2 * i + k) * P:(2 * i + k + 1) * P] for k in range(2) for t in range(TT)], s_turn)

            def out_unit(l, i):
                pe.wait_ge(s_act_lo, l * N_TURN + turn_no("mix", i))
                if i == 0:
                    pe.wait_ge(s_pj, (l + 1) * N_MM)
                down(l, OUT_UNIT + i, t_hi[:, 2 * i:2 * i + 2, :], t_lo[:, 2 * i:2 * i + 2, :],
                     i == 0, i == KT // 2 - 1, i == KT // 2 - 1)

            def up(l, j, t):
                n = l * N_FF + j
                if j:
                    pe.wait_ge(s_m, 2 * n - 1 + t)
                else:
                    pe.wait_ge(s_act_lo, l * N_TURN + turn_no("h2", 2 * t + 1))
                for k in range(KT):
                    U = l * UNITS + up_unit(j) + k // 4
                    if t == 0 and k % 4 == 0:
                        pe.wait_ge(s_lo, U + 1)
                    a = (k % 4) * 512
                    ins = product(ps[:, QKT + t, :], t_hi[:, k, t * P:(t + 1) * P], t_lo[:, k, t * P:(t + 1) * P],
                                  w_hi[:, U % RING, a:a + 512], w_lo[:, U % RING, a:a + 512], k == 0, k == KT - 1)
                    if t == 1 and k == 3:
                        ins.then_inc(s_used, 1)
                ins.then_inc(s_up, 1)

            def turn_m(l, j, t):
                pe.wait_ge(s_m, 2 * (l * N_FF + j) + t + 1)
                pe.wait_ge(s_act_lo, l * N_TURN + (turn_no("m", 2 * (j - 1) + t) if j else turn_no("h2", 2 + t)))
                if j == 3 + t * 0 and j in (3, 6, 9) or (t == 1 and j in (3, 6, 9)):
                    pass
                if j in (3, 6, 9) and (j == 3 or l + 1 < DEPTH):
                    pe.wait_ge(s_table, 4 + 12 * l + 6 + 2 * ((j - 3) // 3) + t + 1)
                turn(ps[:, PTB + t, :], [ffn_m[:, t, k * P:(k + 1) * P] for k in range(2)], s_turn)

            def down_unit_j(l, j):
                pe.wait_ge(s_act_lo, l * N_TURN + turn_no("m", 2 * j + 1))
                if j == 0:
                    pe.wait_ge(s_xup, 4 * l + 2)
                down(l, down_unit(j), m_hi[:, j % 2, :, :], m_lo[:, j % 2, :, :], j == 0, j == N_FF - 1, j == N_FF - 1)

            pe.wait_ge(s_ones, 1)
            pe.wait_ge(s_const, 32)
            for half in range(2):
                sum_modulation(0, half, PTB + half, acc)
            for half in range(2):
                sum_modulation(1, half, QKT + half, gate_t)
            pe.wait_ge(s_table, 4)

            for l in range(DEPTH):
                n_part = 2 + l * PARTS
                turn_h(l, "h1", 0, 4 * l + 1)
                project(l, 0, 0)
                project(l, 1, 0)
                turn_h(l, "h1", 1, 4 * l + 2)
                project(l, 0, 1)
                project(l, 1, 1)
                for s in range(2, N_CHUNK + 3):
                    if s < N_CHUNK:
                        project(l, s, 0)
                    if s == 2:
                        turn_index(l)
                    elif s - 1 < N_CHUNK:
                        turn_qk(l, s - 1)
                    if is_pair(s - 3):
                        weigh_values(l, s - 3, 1)
                    if is_head(s - 2):
                        turn_prob(l, vhead(s - 2))
                    if is_pair(s - 2):
                        scores(l, s - 2, 1)
                    if s in (3, 4):
                        index_logits(l, 2 * (s - 3) + 1)
                    if s < N_CHUNK:
                        project(l, s, 1)
                    if s == N_CHUNK:
                        turn_mixed(l, 0)
                    if s == N_CHUNK + 2:
                        out_unit(l, 2)
                        turn_mixed(l, 3)
                        out_unit(l, 3)
                    if is_head(s - 1):
                        scores(l, s - 1, 0)
                    if is_head(s - 2):
                        weigh_values(l, s - 2, 0)
                    if is_pair(s - 2):
                        turn_prob(l, vhead(s - 2, 1))
                    if s in (2, 3):
                        index_logits(l, 2 * (s - 2))
                    if s in (4, 8, 12):
                        for half in range(2):
                            if half == 0:
                                pe.wait_ge(s_qkT, l * N_QT + s - 2)
                            elif s > 4:
                                pe.wait_ge(s_pT, l * HEADS + s - 4)
                            sum_modulation(n_part + s // 4 - 1, half, (QKT, PTB)[half], acc)
                    if s in (N_CHUNK, N_CHUNK + 1):
                        turn_mixed(l, s - N_CHUNK + 1)
                        out_unit(l, s - N_CHUNK)

                for t in range(TT):
                    turn_h(l, "h2", t, 4 * l + 3 + t)
                for j in range(N_FF):
                    i = {3: 3, 6: 4, 9: 5}.get(j)
                    if i and i > 3 and l + 1 == DEPTH:
                        i = None
                    up(l, j, 0)
                    if j:
                        turn_m(l, j - 1, 1)
                    if i:
                        sum_modulation(n_part + i, 0, PTB, acc)
                    up(l, j, 1)
                    turn_m(l, j, 0)
                    if j:
                        down_unit_j(l, j - 1)
                    if i:
                        sum_modulation(n_part + i, 1, PTB + 1, acc)
                turn_m(l, N_FF - 1, 1)
                down_unit_j(l, N_FF - 1)


_INS = ("x_in", "c_in", "pos_in", "const_in", "w_ada", "b_ada", "gains", "w_stream")


def laid_out(x, c, positions, w_ada, b_ada, g_pre_mix, g_post_mix, w_in, w_out, g_pre_ffn, g_post_ffn,
             w_gate, w_up, w_down):
    f = lambda a: np.asarray(a)
    w_in, w_out, w_gate, w_up, w_down = map(f, (w_in, w_out, w_gate, w_up, w_down))
    sizes = (D, D, D, D, KV_HEADS * DH, KV_HEADS * DH, IH * IDH, IDH, IH, D, D)
    qa, ka, va, qb, kb, vb, qi, ki, wi, ga, gb, end = np.concatenate([[0], np.cumsum(sizes)])
    head = lambda base, h: list(range(base + h * DH, base + (h + 1) * DH))
    chunks = [list(range(ki, wi + IH)), list(range(qi, qi + IH * IDH)), list(range(kb, kb + 512))]
    chunks += [head(qa, h) + head(ka, h) + head(va, h) + head(ga, h) for h in range(8)]
    chunks += [head(qb, h) + head(gb, h) + head(qb, h + 1) + head(gb, h + 1) for h in range(0, 8, 2)]
    stream = np.zeros((DEPTH, UNITS, P, UNIT), np.float32)
    for l in range(DEPTH):
        def put(u, rows):
            k = rows.shape[0] // P
            flat = rows.reshape(k, P, -1).transpose(1, 0, 2).reshape(P, -1)
            stream[l, u, :, :flat.shape[1]] = flat

        put(0, w_in[l][:, chunks[0]])
        for n in range(1, N_CHUNK):
            for i, u in enumerate(chunk_units(n)):
                put(u, w_in[l][i * 512:(i + 1) * 512, chunks[n]])
        for i in range(KT // 2):
            put(OUT_UNIT + i, w_out[l][256 * i:256 * i + 256])
        for j in range(N_FF):
            both = np.concatenate([w_gate[l][:, 256 * j:256 * j + 256], w_up[l][:, 256 * j:256 * j + 256]], axis=1)
            for i in range(2):
                put(up_unit(j) + i, both[i * 512:(i + 1) * 512])
            put(down_unit(j), w_down[l][256 * j:256 * j + 256])
    const = np.zeros((P, N_CONST), np.float32)
    const[:, 0:P] = np.eye(P)
    past = np.arange(P)[None, :] <= np.arange(P)[:, None]
    const[:, P:2 * P] = np.where(past, 0.0, NEG)
    const[:, 3 * P:4 * P] = np.where(past, 0.0, NEG)
    const[:, 4 * P:] = (THETA ** (-np.arange(HALF) / HALF)).astype(np.float32)
    return {
        "x_in": f(x).reshape(TT, P, D).transpose(1, 0, 2),
        "c_in": f(c).reshape(KT, P).T,
        "pos_in": f(positions).reshape(TT, P).T,
        "const_in": const,
        "w_ada": f(w_ada),
        "b_ada": f(b_ada),
        "gains": np.stack([f(g_pre_mix), f(g_post_mix), f(g_pre_ffn), f(g_post_ffn)]),
        "w_stream": stream,
    }


def kernel(**inputs):
    import concourse.bacc as bacc
    from concourse.bass_utils import run_bass_kernel_spmd

    nc = bacc.Bacc("TRN2", target_bir_lowering=False, num_devices=1)
    arrays = {k: np.ascontiguousarray(v) for k, v in laid_out(**inputs).items()}
    args = [nc.dram_tensor(n, arrays[n].shape, mybir.dt.from_np(arrays[n].dtype), kind="ExternalInput").ap() for n in _INS]
    out = nc.dram_tensor("out", (TT, P, D), F32, kind="ExternalOutput").ap()
    hybrid_decoder_trunk(nc, *args, out)
    r = run_bass_kernel_spmd(nc, [arrays], core_ids=[0])
    return r.results[0]["out"].reshape(1, SEQ, D)
```

```python
from contextlib import ExitStack

import numpy as np

import concourse.bass as bass
from concourse import mybir

P = 128
D = 1024
SEQ = 256
DEPTH = 2
TT = SEQ // P
KT = D // P
DH = 128
HALF = DH // 4 // 2
IH, IDH = 8, 64
IHALF = IDH // 4 // 2
FF = 2816
N_TOP = SEQ // 4
THETA = 500000.0
EPS = 1e-6
NEG = -1e30
TAKEN = -3e38
SCALE = DH ** -0.5
KV_HEADS = 2

UNIT = 2048
SMALL = IDH + IH
N_CHUNK = 15
FIRST_HEAD = 3
HEAD_CHUNKS = ([(False, h) for h in range(4)] + [(True, 0), (False, 4), (True, 2), (False, 5)]
               + [(True, 4), (False, 6), (True, 6), (False, 7)])
N_FF = FF // 256
OUT_UNIT = 1 + 2 * (N_CHUNK - 1)
FFN_UNIT = OUT_UNIT + KT // 2
UNITS = FFN_UNIT + 3 * N_FF
RAW, RING = 3, 5
PIECE = 1024
PARTS = 6
ADA_RING = 2
START = 2 * KT
START_ORDER = (8, 0, 9, 1, 10, 2, 11, 3, 12, 4, 13, 5, 6, 7, 14, 15)
PRO_OTHER = START - 2 * ADA_RING
N_CONST = P + 3 * P + HALF

F32 = mybir.dt.float32
F32R = mybir.dt.float32r
I32 = mybir.dt.int32
ALU = mybir.AluOpType
ACT = mybir.ActivationFunctionType

SH1, SC1, GT1, SH2, SC2, GT2 = range(6)


def up_unit(j):
    return FFN_UNIT + (3 * j - 1 if j else 0)


def down_unit(j):
    return FFN_UNIT + (3 * j + 4 if j < N_FF - 1 else 3 * j + 2)


def chunk_units(c):
    return [0] if c == 0 else [2 * c - 1, 2 * c]


def two_pi_parts():
    rest, parts = 2 * np.pi, []
    for low in (9, 21, 33, 45):
        part = np.floor(rest * 2.0 ** low) / 2.0 ** low
        parts.append(float(part))
        rest -= part
    return parts


RSQRT_BITS = float(0x5F3759DF - 2 ** 22 - 2 ** 31)
NEWTON = 3
ROUND = 1.5 * 2.0 ** 23
PI_IN = 3.1415925

SPLITS = {2: [u + RING for u in (0, 1, 2)]} | {s: [u + RING for u in chunk_units(s - 1)] for s in range(3, N_CHUNK + 1)} \
    | {N_CHUNK + 1: [OUT_UNIT + RING], N_CHUNK + 2: [OUT_UNIT + 1 + RING]}

MADE = [(0, SC1), (0, SH1)] + [p for l in range(DEPTH) for p in (
    (l, GT1), (l, SC2), (l, SH2), (l, GT2), (l + 1, SC1), (l + 1, SH1))][:PARTS * DEPTH - 2]
MIX_PIECES = {1: (2, 0)} | {s: (1, 1) for s in (2, 3, 4)} | {s: (1, 0) for s in (5, 6, 7, 8)} \
    | {s: (1, 1) for s in range(9, 14)} | {14: (1, 1)}
MIX_TABLES = (5, 11)
TOP_STEPS = range(5, 9)


def ffn_pieces(l):
    if l + 1 < DEPTH:
        return (3, 2, 3, 2, 3, 2, 3, 2, 2, 2, 0), (4, 8)
    return (1, 1, 1, 1, 1, 1, 1, 1, 0, 0, 0), (9,)


def up_splits(j):
    ahead = [OUT_UNIT + 2 + RING, OUT_UNIT + 3 + RING] if j == 0 else [down_unit(j - 2) + RING] if j > 1 else []
    return ahead, [up_unit(j) + RING, up_unit(j) + 1 + RING]


ATTENDED = [(dsa, h + b) for dsa, h in HEAD_CHUNKS for b in range(1 + dsa)]
HEADS = len(ATTENDED)


def hybrid_decoder_trunk(nc, x_in, c_in, pos_in, const_in, w_ada, b_ada, gains, w_stream, out):
    with ExitStack() as ctx:
        def sb(name, shape, dt=F32):
            return ctx.enter_context(nc.sbuf_tensor(name, shape, dt))

        def sem(name):
            return ctx.enter_context(nc.semaphore(name))

        ps = ctx.enter_context(nc.psum_tensor("ps", [P, 8, 512], F32))
        QKT, SCO, PTB, OUT = 4, 5, 6, 7

        raw = sb("raw", [P, RAW, UNIT])
        w_hi = sb("w_hi", [P, RING, UNIT], F32R)
        w_lo = sb("w_lo", [P, RING, UNIT], F32R)
        ada = sb("ada", [P, ADA_RING, PIECE])

        x = sb("x", [P, TT, D])
        t_hi = sb("t_hi", [P, KT, SEQ], F32R)
        t_lo = sb("t_lo", [P, KT, SEQ], F32R)
        mixed = sb("mixed", [P, TT, D])
        scale_t = sb("scale_t", [P, D])
        shift_t = sb("shift_t", [P, D])
        gate_t = sb("gate_t", [P, D])
        acc = sb("acc", [P, D])
        tables = (gate_t, scale_t, shift_t)

        pj = sb("pj", [P, 3, TT, 512])
        hbuf = pj[:, :, :, :].rearrange("p b t n -> p b (t n)")
        junk = hbuf[:, 2, :]
        kiw = sb("kiw", [P, TT, SMALL])
        kid = sb("kid", [P, TT, 2, IDH])
        kiT = sb("kiT", [P, SEQ])
        region = sb("region", [P, 4 * SEQ])
        qiT = region[:, :].rearrange("p (b n) -> p b n", b=4)
        sx = region[:, 0:3 * P]
        prob = region[:, 3 * P:6 * P]
        qkT = sb("qkT", [P, 512])
        kbT = sb("kbT", [P, 512])
        wide_c = (qkT, kbT)
        vb = sb("vb", [P, TT, 256])
        relu = sb("relu", [P, 2, 3 * P])
        probT = relu[:, 0, :]
        ffn_s = relu[:, :, 0:256]
        score = sb("score", [P, 3 * P])
        keep = sb("keep", [P, 3 * P])
        ffn_m = sb("ffn_m", [P, TT, 256])
        m_hi = sb("m_hi", [P, 2, 2, SEQ], F32R)
        m_lo = sb("m_lo", [P, 2, 2, SEQ], F32R)
        rope_a, rope_b = ffn_m[:, 0, :], ffn_m[:, 1, :]

        const = sb("const", [P, N_CONST])
        ident = const[:, 0:P]
        causal = const[:, P:4 * P]
        inv_freq = const[:, 4 * P:4 * P + HALF]
        ones = sb("ones", [P, P])
        pos = sb("pos", [P, TT], I32)
        cT = sb("cT", [P, KT])
        cs = sb("cs", [P, KT])
        posf = sb("posf", [P, TT])
        ang = sb("ang", [P, 7, TT, HALF])
        cos_t = sb("cos_t", [P, TT, 2 * HALF])
        sin_t = sb("sin_t", [P, TT, 2 * HALF])
        icos_t = sb("icos_t", [P, TT, 2 * IHALF])
        isin_t = sb("isin_t", [P, TT, 2 * IHALF])
        wis = sb("wis", [P, TT, IH])
        gtmp = kiT[:, :].rearrange("p (t n) -> p t n", t=TT)
        max8 = sb("max8", [P, 2, 8])
        ssq = sb("ssq", [P, TT])
        rstd = sb("rstd", [P, TT])
        rms = sb("rms", [P, TT, 2])
        nmax = sb("nmax", [P, 2, TT])
        rsum = sb("rsum", [P, 2, TT])
        rinv = sb("rinv", [P, TT])

        s_c = sem("c_landed")
        s_const = sem("const_landed")
        s_x = sem("x_landed")
        s_raw = [sem(f"raw_landed{i}") for i in range(RAW)]
        s_ada = [sem(f"ada_landed{i}") for i in range(ADA_RING)]
        s_bias = [sem(f"bias_landed{i}") for i in range(3)]
        s_bias0 = [sem(f"first_bias_landed{i}") for i in range(2)]
        s_gain0 = sem("first_gain_landed")
        s_gain = sem("gain_landed")
        s_pro = [sem(f"start_piece_landed{i}") for i in range(PRO_OTHER)]
        s_out = sem("out_stored")
        s_zero = sem("sum_zeroed")
        s_shift = sem("shift_table")
        s_reduced = sem("modulation_reduced")
        s_ang = sem("angles")
        s_rope_t = sem("rotary_tables")
        s_pool = sem("pool_chain")
        s_rstd = sem("rstd_ready")
        s_cs = sem("silu_c")
        s_sin = sem("sines")
        s_hi = sem("hi_split")
        s_pj = sem("pj_copied")
        s_iqk = sem("index_qk_copied")
        s_qkT = sem("qkT_copied")
        s_relu = sem("logits_rectified")
        s_exp = sem("exp_done")
        s_pT = sem("probT_copied")
        s_act_hi = sem("act_hi_split")
        s_sq = sem("squares_summed")
        s_silu = sem("silu_done")
        s_lo = sem("lo_split")
        s_roped = sem("roped")
        s_iacc = sem("index_summed")
        s_ttr = sem("masked_min")
        s_gated = sem("head_gated")
        s_act_lo = sem("act_lo_split")
        s_h = sem("h_ready")
        s_xup = sem("x_updated")
        s_m = sem("m_ready")
        s_adause = sem("ada_used")
        s_table = sem("table_made")
        s_dve = sem("dve_chain")
        s_ones = sem("ones_set")
        s_wide = sem("wide_c_made")
        s_mm = sem("projected")
        s_used = sem("unit_used")
        s_iT = sem("index_turned")
        s_qT = sem("qk_turned")
        s_logit = sem("index_logits")
        s_sco = sem("scores")
        s_prT = sem("prob_turned")
        s_av = sem("head_out")
        s_turn = sem("act_turned")
        s_y = sem("sublayer_out")
        s_up = sem("up_projected")
        s_adasum = sem("modulation_summed")
        s_fed = sem("shift_piece_used")

        N_MM, N_ROPE, N_QT, N_TURN = 2 * N_CHUNK, N_CHUNK, N_CHUNK - 2, 12 + 2 * N_FF

        start_at = ([ada[:, i, :] for i in range(ADA_RING)] + [mixed[:, t, :] for t in range(TT)]
                    + [hbuf[:, i, :] for i in range(3)] + [region[:, :]]
                    + [raw[:, i // 2, (i % 2) * PIECE:(i % 2 + 1) * PIECE] for i in range(2 * RAW)])

        def piece_at(n):
            if n < ADA_RING:
                return start_at[n], s_ada[n], 16
            if n < START - ADA_RING:
                return start_at[n], s_pro[n - ADA_RING], 16
            return ada[:, n % ADA_RING, :], s_ada[n % ADA_RING], 16 * (2 + (n - START + ADA_RING) // ADA_RING)

        def mm_no(c, t):
            return 2 * t + c + 1 if c < 2 else 2 * c + t + 1

        def turn_no(kind, i):
            return {"h1": 0, "mix": 4, "h2": 8, "m": 12}[kind] + i + 1

        def is_head(c):
            return FIRST_HEAD <= c < N_CHUNK

        def is_pair(c):
            return is_head(c) and HEAD_CHUNKS[c - FIRST_HEAD][0]

        def vhead(c, b=0):
            dsa, h = HEAD_CHUNKS[c - FIRST_HEAD]
            return ATTENDED.index((dsa, h + b))

        def last_head(c):
            return vhead(c, 1 if is_pair(c) else 0)

        used_units = ([chunk_units(c)[0] for c in range(1, N_CHUNK)] + [OUT_UNIT + i for i in range(KT // 2 - 1)]
                      + sorted([up_unit(j) for j in range(N_FF)] + [down_unit(j) for j in range(N_FF - 1)]))
        N_USED = len(used_units)

        def wait_multiplied(eng, U):
            l, u = U // UNITS, U % UNITS
            if u in used_units:
                eng.wait_ge(s_used, l * N_USED + used_units.index(u) + 1)
            elif u < OUT_UNIT:
                eng.wait_ge(s_mm, l * N_MM + mm_no(u // 2, 1))
            elif u == FFN_UNIT - 1:
                eng.wait_ge(s_y, 4 * l + 2)
            elif u == UNITS - 1:
                eng.wait_ge(s_y, 4 * l + 4)
            else:
                j = [up_unit(j) + 1 for j in range(N_FF)].index(u)
                eng.wait_ge(s_up, 2 * (l * N_FF + j) + 2)

        block = ctx.enter_context(nc.Block())

        @block.sync
        def _(sp):
            pieces = [0]

            def load_unit(l, u):
                U = l * UNITS + u
                if U >= DEPTH * UNITS:
                    return
                if U >= RAW:
                    sp.wait_ge(s_lo, U - RAW + 1)
                n = KT * SMALL if U % UNITS == 0 else UNIT
                sp.dma_start(raw[:, U % RAW, 0:n], w_stream[U // UNITS, U % UNITS, :, 0:n]).then_inc(s_raw[U % RAW], 16)

            def load_pieces(count):
                for _ in range(count):
                    n = START_ORDER[pieces[0]] if pieces[0] < START else pieces[0]
                    l, part = MADE[n // KT]
                    dst, landed, _ = piece_at(n)
                    if n >= START + ADA_RING:
                        sp.wait_ge(s_adause, n - KT - ADA_RING + 1)
                    elif n >= START:
                        sp.wait_ge(s_fed, n - KT - ADA_RING + 1)
                    elif n >= START - ADA_RING:
                        sp.wait_ge(s_adause, n - START + ADA_RING + 1)
                    k = n % KT
                    sp.dma_start(dst, w_ada[l, k * P:(k + 1) * P, part * D:(part + 1) * D]).then_inc(landed, 16)
                    pieces[0] += 1

            sp.dma_start(cT[:], c_in).then_inc(s_c, 16)
            load_pieces(2)
            sp.dma_start(const[:], const_in).then_inc(s_const, 16)
            sp.dma_start(pos[:], pos_in).then_inc(s_const, 16)
            load_pieces(10)
            sp.dma_start(x[:, :, :], x_in).then_inc(s_x, 16)
            load_pieces(4)
            for u in range(RAW):
                sp.wait_ge(s_fed, 2 * u + 2)
                load_unit(0, u)
            for l in range(DEPTH):
                for u in range(RAW, RING):
                    load_unit(l, u)
                load_pieces(sum(MIX_PIECES[1]))
                for s in range(2, N_CHUNK + 3):
                    for half in range(2):
                        for u in SPLITS[s][:-1] if half == 0 else SPLITS[s][-1:]:
                            load_unit(l, u)
                        if s in MIX_PIECES:
                            load_pieces(MIX_PIECES[s][half])
                for j in range(N_FF):
                    ahead, behind = up_splits(j)
                    many = ffn_pieces(l)[0][j]
                    for u in ahead + behind[:1]:
                        load_unit(l, u)
                    load_pieces(min(many, 1))
                    load_unit(l, behind[1])
                    load_pieces(max(many - 1, 0))
            for t in range(TT):
                sp.wait_ge(s_xup, 4 * (DEPTH - 1) + 3 + t)
                sp.dma_start(out[t], x[:, t, :]).then_inc(s_out, 16)
            sp.wait_ge(s_out, 16 * TT)

        @block.gpsimd
        def _(pool):
            links = [0]

            def link(ins):
                ins.then_inc(s_pool, 1)
                links[0] += 1
                pool.wait_ge(s_pool, links[0])

            zeroed = [0]

            def seed(buf, l, part, landed):
                nc.gpsimd.memset(buf[:, :], 0.0).then_inc(s_zero, 1)
                zeroed[0] += 1
                pool.wait_ge(s_zero, zeroed[0])
                pool.dma_start(buf[0:1, :], b_ada[l:l + 1, part * D:(part + 1) * D]).then_inc(landed, 16)

            def reduce(n, i):
                pool.wait_ge(s_adause, KT * n)
                nc.gpsimd.partition_all_reduce(acc[:, :], tables[i][:, :], P, bass.bass_isa.ReduceOp.add).then_inc(s_reduced, 1)
                pool.wait_ge(s_reduced, n - 1)

            def finish(n, i, l, which):
                reduce(n, i)
                pool.dma_start(tables[i][:, :], gains[which, l:l + 1, :].broadcast_to([P, D])).then_inc(s_gain, 16)

            def finish_shift(n, done):
                reduce(n, 2)
                nc.gpsimd.tensor_copy(shift_t[:, :], acc[:, :]).then_inc(s_shift, 1)
                pool.wait_ge(s_shift, done)

            def wait_norm_used(eng, n):
                t = n % 2
                l, i = (n - 2) // 8, (n - 2) % 8 // 2
                if i in (0, 2):
                    eng.wait_ge(s_xup, 4 * l + i + t + 1)
                else:
                    eng.wait_ge(s_h, 8 * l + (4 if i == 1 else 8) + 2 * t + 2)

            def inverse_rms(n):
                t = n % 2
                u, y, e = rms[:, t, 0:1], rstd[:, t:t + 1], rms[:, t, 1:2]
                pool.wait_ge(s_sq, n + 1)
                if n > 1:
                    wait_norm_used(pool, n - 2)
                link(nc.gpsimd.tensor_scalar(u, ssq[:, t:t + 1], EPS, 0.5, ALU.add, ALU.mult))
                link(nc.gpsimd.tensor_scalar(y.bitcast(I32), u.bitcast(I32), -0.5, RSQRT_BITS, ALU.mult, ALU.add))
                for step in range(NEWTON):
                    link(nc.gpsimd.tensor_scalar(e, y, u, y, ALU.mult, ALU.mult))
                    ins = nc.gpsimd.tensor_scalar(y, e, 1.5, y, ALU.subtract, ALU.mult)
                    if step < NEWTON - 1:
                        link(ins)
                ins.then_inc(s_rstd, 1)

            seed(acc, 0, SC1, s_bias0[0])
            seed(gate_t, 0, SH1, s_bias0[1])
            pool.dma_start(scale_t[:, :], gains[0, 0:1, :].broadcast_to([P, D])).then_inc(s_gain0, 16)

            pool.wait_ge(s_const, 32)
            link(nc.gpsimd.tensor_copy(posf[:, :], pos[:, :]))
            th, turns, r, quarter, high, low, part = (ang[:, i] for i in range(7))
            for t in range(TT):
                ins = nc.gpsimd.tensor_scalar(th[:, t, :], inv_freq, posf[:, t:t + 1], None, ALU.mult)
            link(ins)
            link(nc.gpsimd.tensor_scalar(turns, th, 1.0 / (2 * np.pi), ROUND, ALU.mult, ALU.add))
            link(nc.gpsimd.tensor_scalar(turns, turns, -ROUND, None, ALU.add))
            link(nc.gpsimd.tensor_scalar(high, turns, ROUND * 2.0 ** 11, None, ALU.add))
            link(nc.gpsimd.tensor_scalar(high, high, -ROUND * 2.0 ** 11, None, ALU.add))
            link(nc.gpsimd.tensor_tensor(low, turns, high, ALU.subtract))
            parts = two_pi_parts()
            for which, i in ((high, 0), (low, 0), (high, 1), (low, 1), (high, 2), (low, 2), (high, 3)):
                link(nc.gpsimd.tensor_scalar(part, which, parts[i], None, ALU.mult))
                link(nc.gpsimd.tensor_tensor(r, th if which is high and i == 0 else r, part, ALU.subtract))
            link(nc.gpsimd.tensor_scalar(r, r, PI_IN, -PI_IN, ALU.min, ALU.max))
            link(nc.gpsimd.tensor_scalar(quarter, r, np.pi / 2, None, ALU.add))
            link(nc.gpsimd.tensor_scalar(turns, quarter, np.pi, -2 * np.pi, ALU.is_gt, ALU.mult))
            link(nc.gpsimd.tensor_tensor(quarter, quarter, turns, ALU.add))
            nc.gpsimd.tensor_scalar(quarter, quarter, PI_IN, -PI_IN, ALU.min, ALU.max).then_inc(s_ang, 1)
            for t in range(TT):
                inverse_rms(t)
            pool.wait_ge(s_sin, 1)
            sine, cosine = ang[:, 4], ang[:, 5]
            for w, c_t, s_t, step in ((HALF, cos_t, sin_t, 1), (IHALF, icos_t, isin_t, HALF // IHALF)):
                for i in range(2):
                    nc.gpsimd.tensor_copy(c_t[:, :, i * w:(i + 1) * w], cosine[:, :, ::step])
                nc.gpsimd.tensor_copy(s_t[:, :, 0:w], sine[:, :, ::step])
                ins = nc.gpsimd.tensor_scalar(s_t[:, :, w:], sine[:, :, ::step], -1.0, None, ALU.mult)
            ins.then_inc(s_rope_t, 1)

            pool.wait_ge(s_adasum, 3)
            for l in range(DEPTH):
                n = 2 + l * PARTS
                if l:
                    pool.wait_ge(s_xup, 4 * l)
                seed(gate_t, l, GT1, s_bias[0])
                pool.wait_ge(s_h, 8 * l + 4)
                seed(scale_t, l, SC2, s_bias[1])
                seed(shift_t, l, SH2, s_bias[2])
                finish(n, 0, l, 1)
                pool.wait_ge(s_table, 2 + 4 * l + 1)
                finish(n + 1, 1, l, 2)
                pool.wait_ge(s_table, 2 + 4 * l + 2)
                finish_shift(n + 2, 2 * l + 1)
                for i in range(4):
                    inverse_rms(2 + 8 * l + i)
                more = l + 1 < DEPTH
                pool.wait_ge(s_xup, 4 * l + 2)
                seed(gate_t, l, GT2, s_bias[0])
                if more:
                    pool.wait_ge(s_h, 8 * l + 8)
                    seed(scale_t, l + 1, SC1, s_bias[1])
                    seed(shift_t, l + 1, SH1, s_bias[2])
                finish(n + 3, 0, l, 3)
                if more:
                    pool.wait_ge(s_table, 2 + 4 * l + 3)
                    finish(n + 4, 1, l + 1, 0)
                    pool.wait_ge(s_table, 2 + 4 * l + 4)
                    finish_shift(n + 5, 2 * l + 2)
                for i in range(4 if more else 2):
                    inverse_rms(6 + 8 * l + i)

        @block.scalar
        def _(act):
            def split_hi(l, u):
                U = l * UNITS + u
                if U >= DEPTH * UNITS:
                    return
                n = KT * SMALL if U % UNITS == 0 else UNIT
                act.wait_ge(s_raw[U % RAW], 16 * (U // RAW + 1))
                if U >= RING:
                    wait_multiplied(act, U - RING)
                nc.scalar.activation(w_hi[:, U % RING, 0:n], raw[:, U % RAW, 0:n], ACT.Copy).then_inc(s_hi, 1)

            def copy_chunk(l, c, t):
                act.wait_ge(s_mm, l * N_MM + mm_no(c, t))
                src = ps[:, (c % 2) + 2 * t, :]
                if c == 0:
                    nc.scalar.activation(kiw[:, t, :], src[:, 0:SMALL], ACT.Copy).then_inc(s_pj, 1)
                    return
                dst = pj[:, c % 3, t, :]
                if c == 1:
                    act.wait_ge(s_turn, l * N_TURN + turn_no("h1", 3))
                elif c == 4:
                    act.wait_ge(s_iT, l * 3 + 3)
                elif c == 5:
                    act.wait_ge(s_qT, l * N_QT + 1)
                elif c > 5:
                    act.wait_ge(s_gated, l * HEADS + last_head(c - 3) + 1)
                if c == 1:
                    nc.scalar.activation(dst, src, ACT.Copy).then_inc(s_pj, 1)
                elif c == 2:
                    nc.scalar.activation(dst[:, 0:256], src[:, 0:256], ACT.Copy)
                    nc.scalar.activation(vb[:, t, :], src[:, 256:512], ACT.Copy).then_inc(s_pj, 1)
                elif not is_pair(c):
                    nc.scalar.activation(dst[:, 0:384], src[:, 0:384], ACT.Copy)
                    nc.scalar.activation(dst[:, 384:512], src[:, 384:512], ACT.Tanh, scale=0.5).then_inc(s_pj, 1)
                else:
                    d = dst.rearrange("p (h a n) -> p h a n", h=2, a=2)
                    q = src.rearrange("p (h a n) -> p h a n", h=2, a=2)
                    nc.scalar.activation(d[:, :, 0, :], q[:, :, 0, :], ACT.Copy)
                    nc.scalar.activation(d[:, :, 1, :], q[:, :, 1, :], ACT.Tanh, scale=0.5).then_inc(s_pj, 1)

            def softmax_exp(l, v):
                n = l * HEADS + v
                act.wait_ge(s_ttr, n + 1)
                if n:
                    act.wait_ge(s_prT, n)
                if n > 1:
                    act.wait_ge(s_gated, n - 1)
                nc.scalar.activation(prob[:, 0:P], sx[:, 0:P], ACT.Exp, bias=nmax[:, v % 2, 0:1], scale=-1.0,
                                     accum_out=rsum[:, v % 2, 0:1])
                nc.scalar.activation(prob[:, P:3 * P], sx[:, P:3 * P], ACT.Exp, bias=nmax[:, v % 2, 1:2], scale=-1.0,
                                     accum_out=rsum[:, v % 2, 1:2]).then_inc(s_exp, 1)

            def copy_probT(l, v):
                act.wait_ge(s_prT, l * HEADS + v + 1)
                if v:
                    act.wait_ge(s_av, l * HEADS + v)
                else:
                    act.wait_ge(s_iacc, 4 * l + 4)
                nc.scalar.activation(probT, ps[:, PTB, 0:3 * P], ACT.Copy).then_inc(s_pT, 1)

            def copy_qkT(l, c):
                act.wait_ge(s_qT, l * N_QT + c - 1)
                if c == 2:
                    nc.scalar.activation(kbT[:, :], ps[:, QKT, :], ACT.Copy).then_inc(s_qkT, 1)
                    return
                if c > FIRST_HEAD:
                    act.wait_ge(s_sco, l * HEADS + last_head(c - 1) + 1)
                nc.scalar.activation(qkT[:, :], ps[:, QKT, :], ACT.Copy).then_inc(s_qkT, 1)

            def copy_index(l):
                act.wait_ge(s_iT, l * 3 + 1)
                nc.scalar.activation(kiT[:, :], ps[:, OUT, 0:SEQ], ACT.Copy).then_inc(s_iqk, 1)
                for i, bank in enumerate((QKT, PTB)):
                    act.wait_ge(s_iT, l * 3 + 2 + i)
                    nc.scalar.activation(region[:, 512 * i:512 * i + 512], ps[:, bank, :], ACT.Copy).then_inc(s_iqk, 1)

            def rectify(l, i):
                act.wait_ge(s_logit, 4 * l + i + 1)
                if i:
                    act.wait_ge(s_iacc, 4 * l + i)
                for b, bank in enumerate((SCO, OUT)):
                    ins = nc.scalar.activation(relu[:, b, :], ps[:, bank, 0:3 * P], ACT.Relu, scale=float(IDH) ** -0.5)
                ins.then_inc(s_relu, 1)

            def act_hi(l, kind, i, dst, src):
                act.wait_ge(s_turn, l * N_TURN + turn_no(kind, i))
                nc.scalar.activation(dst, src, ACT.Copy).then_inc(s_act_hi, 1)

            def h_hi(l, kind, t):
                for i in range(2):
                    act_hi(l, kind, 2 * t + i, t_hi[:, 4 * i:4 * i + 4, t * P:(t + 1) * P],
                           ps[:, PTB + i, :].rearrange("p (k n) -> p k n", k=4))

            def mix_hi(l, i):
                act_hi(l, "mix", i, m_hi[:, i % 2, :, :], ps[:, QKT, :].rearrange("p (k n) -> p k n", k=2))

            def m_hi_split(l, j, t):
                act_hi(l, "m", 2 * j + t, m_hi[:, j % 2, :, t * P:(t + 1) * P],
                       ps[:, PTB + t, 0:256].rearrange("p (k n) -> p k n", k=2))

            def sum_squares(n, t, src):
                if n >= 2:
                    act.wait_ge(s_rstd, n - 1)
                if n:
                    act.wait_ge(s_sq, n)
                dst = junk if n >= 2 else ps[:, 0:2, :].rearrange("p b n -> p (b n)")
                nc.scalar.activation(dst, src, ACT.Square, scale=float(D) ** -0.5,
                                     accum_out=ssq[:, t:t + 1]).then_inc(s_sq, 1)

            def border(l, mid):
                n = 2 + 8 * l + (0 if mid else 4)
                for t in range(TT):
                    act.wait_ge(s_y, 4 * l + (0 if mid else 2) + t + 1)
                    sum_squares(n + t, t, ps[:, 2 * t:2 * t + 2, :].rearrange("p b n -> p (b n)"))
                if not mid and l + 1 == DEPTH:
                    return
                for t in range(TT):
                    act.wait_ge(s_xup, 4 * l + (0 if mid else 2) + t + 1)
                    sum_squares(n + 2 + t, t, x[:, t, :])

            act.wait_ge(s_c, 16)
            nc.scalar.activation(cs[:, :], cT[:, :], ACT.Silu).then_inc(s_cs, 1)
            act.wait_ge(s_ang, 1)
            nc.scalar.activation(ang[:, 4:6], ang[:, 2:4], ACT.Sin).then_inc(s_sin, 1)
            act.wait_ge(s_x, 16)
            for t in range(TT):
                sum_squares(t, t, x[:, t, :])
            for u in range(RAW):
                split_hi(0, u)

            for l in range(DEPTH):
                h_hi(l, "h1", 0)
                h_hi(l, "h1", 1)
                copy_chunk(l, 0, 0)
                for u in range(RAW, RING):
                    split_hi(l, u)
                copy_chunk(l, 1, 0)
                for s in range(2, N_CHUNK + 3):
                    if s == 2:
                        copy_chunk(l, 0, 1)
                    if s - 1 < N_CHUNK:
                        copy_chunk(l, s - 1, 1)
                    if is_pair(s - 3):
                        copy_probT(l, vhead(s - 3, 1))
                    for u in SPLITS[s][:-1]:
                        split_hi(l, u)
                    if is_head(s - 2):
                        softmax_exp(l, vhead(s - 2))
                    if s in (3, 4):
                        rectify(l, 2 * (s - 3))
                    if s == 2:
                        copy_index(l)
                    elif s - 1 < N_CHUNK:
                        copy_qkT(l, s - 1)
                    if is_head(s - 2):
                        copy_probT(l, vhead(s - 2))
                    if s == N_CHUNK + 2:
                        mix_hi(l, 3)
                    split_hi(l, SPLITS[s][-1])
                    if is_pair(s - 2):
                        softmax_exp(l, vhead(s - 2, 1))
                    if s in (3, 4):
                        rectify(l, 2 * (s - 3) + 1)
                    if s < N_CHUNK:
                        copy_chunk(l, s, 0)
                    if N_CHUNK - 1 <= s < N_CHUNK + 2:
                        mix_hi(l, s - N_CHUNK + 1)

                border(l, True)
                for t in range(TT):
                    h_hi(l, "h2", t)
                for j in range(N_FF):
                    if j:
                        m_hi_split(l, j - 1, 1)
                    for u in up_splits(j)[0]:
                        split_hi(l, u)
                    for t in range(TT):
                        act.wait_ge(s_up, 2 * (l * N_FF + j) + t + 1)
                        n = l * N_FF + j
                        if n:
                            act.wait_ge(s_m, 2 * n + t - 1)
                        nc.scalar.activation(ffn_s[:, t, :], ps[:, QKT + t, 0:256], ACT.Silu).then_inc(s_silu, 1)
                    m_hi_split(l, j, 0)
                    for u in up_splits(j)[1]:
                        split_hi(l, u)
                m_hi_split(l, N_FF - 1, 1)
                border(l, False)

        @block.vector
        def _(dve):
            links = [0]

            def link(ins):
                ins.then_inc(s_dve, 1)
                links[0] += 1
                dve.wait_ge(s_dve, links[0])

            def split_lo(l, u):
                U = l * UNITS + u
                if U >= DEPTH * UNITS:
                    return
                n = KT * SMALL if U % UNITS == 0 else UNIT
                dve.wait_ge(s_hi, U + 1)
                nc.vector.tensor_tensor(w_lo[:, U % RING, 0:n], raw[:, U % RAW, 0:n],
                                        w_hi[:, U % RING, 0:n].bitcast(F32), ALU.subtract).then_inc(s_lo, 1)

            pieces = [0]

            def add_pieces(many):
                for _ in range(many):
                    m = pieces[0]
                    n = m if m < KT else m + KT
                    k, part = n % KT, n // KT
                    buf = tables[(part - 2) % 3] if part else acc
                    if k == 0:
                        dve.wait_ge(s_bias[(part - 2) % 3] if part else s_bias0[0], 16 * ((part - 2) // 3 + 1) if part else 16)
                    src, landed, count = piece_at(n)
                    dve.wait_ge(landed, count)
                    if m:
                        dve.wait_ge(s_adause, m)
                    nc.vector.scalar_tensor_tensor(out=buf[:, :], in0=src, scalar=cs[:, k:k + 1],
                                                   in1=buf[:, :], op0=ALU.mult, op1=ALU.add).then_inc(s_adause, 1)
                    pieces[0] += 1

            def first_scale(half):
                cols = slice(512 * half, 512 * half + 512)
                dve.wait_ge(s_adasum, half + 1)
                nc.vector.scalar_tensor_tensor(out=scale_t[:, cols], in0=ps[:, PTB + half, :], scalar=1.0,
                                               in1=scale_t[:, cols], op0=ALU.add, op1=ALU.mult).then_inc(s_table, 1)

            def make_table(n):
                table, extra = ((gate_t, 0.0), (scale_t, 1.0))[(n - 1) % 2]
                dve.wait_ge(s_gain, 16 * n)
                nc.vector.scalar_tensor_tensor(out=table[:, :], in0=acc[:, :], scalar=extra, in1=table[:, :],
                                               op0=ALU.add, op1=ALU.mult).then_inc(s_table, 1)

            def rotate(src, dst, heads, width, cos, sin, done):
                half = width // 2
                a = rope_a[:, 0:TT * heads * width].rearrange("p (t h w) -> p t h w", t=TT, h=heads)
                b = rope_b[:, 0:TT * heads * width].rearrange("p (t h w) -> p t h w", t=TT, h=heads)
                for t in range(TT):
                    cb = cos[:, t:t + 1, :].broadcast_to([P, heads, width])
                    sn = sin[:, t:t + 1, :].broadcast_to([P, heads, width])
                    nc.vector.tensor_tensor(a[:, t], src[:, t], cb, ALU.mult)
                    ins = nc.vector.tensor_tensor(b[:, t], src[:, t], sn, ALU.mult)
                link(ins)
                for t in range(TT):
                    x1, x2 = dst[t]
                    h = x1.shape[1]
                    a1 = a[:, t] if h == heads else a[:, t].broadcast_to([P, h, width])
                    b1 = b[:, t] if h == heads else b[:, t].broadcast_to([P, h, width])
                    nc.vector.tensor_tensor(x1, a1[:, :, 0:half], b1[:, :, half:], ALU.add)
                    ins = nc.vector.tensor_tensor(x2, a1[:, :, half:], b1[:, :, 0:half], ALU.add)
                ins.then_inc(s_roped, 1)
                dve.wait_ge(s_roped, done)

            def rope(l, c):
                done = l * N_ROPE + c + 1
                if c == 0 and l == 0:
                    dve.wait_ge(s_rope_t, 1)
                dve.wait_ge(s_pj, l * N_MM + (3 if c == 0 else 2 * c + 2))
                if c == 0:
                    nc.vector.tensor_scalar(wis[:, :, :], kiw[:, :, IDH:], float(IH) ** -0.5, None, ALU.mult)
                    nc.vector.tensor_copy(kid[:, :, 0, :], kiw[:, :, 0:IDH])
                    link(nc.vector.tensor_copy(kid[:, :, 1, :], kiw[:, :, 0:IDH]))
                    src = kiw[:, :, 0:2 * IHALF].rearrange("p t (h w) -> p t h w", h=1)
                    dst = [(kid[:, t, :, 0:IHALF], kid[:, t, :, IHALF:2 * IHALF]) for t in range(TT)]
                    rotate(src, dst, 1, 2 * IHALF, icos_t, isin_t, done)
                    return
                b = pj[:, c % 3, :, :]
                if c == 1:
                    v = b.rearrange("p t (h w) -> p t h w", h=IH)
                    rotate(v[:, :, :, 0:2 * IHALF],
                           [(v[:, t, :, 0:IHALF], v[:, t, :, IHALF:2 * IHALF]) for t in range(TT)],
                           IH, 2 * IHALF, icos_t, isin_t, done)
                    return
                v = b.rearrange("p t (h w) -> p t h w", h=2 if is_pair(c) else 4)[:, :, 0:2, :]
                rotate(v[:, :, :, 0:2 * HALF],
                       [(v[:, t, :, 0:HALF], v[:, t, :, HALF:2 * HALF]) for t in range(TT)],
                       2, 2 * HALF, cos_t, sin_t, done)

            def mask_scores(l, v):
                n = l * HEADS + v
                dve.wait_ge(s_sco, n + 1)
                if n:
                    dve.wait_ge(s_exp, n)
                m = keep if ATTENDED[v][0] else causal
                for t, cols in enumerate((slice(0, P), slice(P, 3 * P))):
                    ins = nc.vector.tensor_tensor_reduce(sx[:, cols], ps[:, SCO, cols], m[:, cols], -SCALE, 3e38,
                                                         ALU.add, ALU.min, nmax[:, v % 2, t:t + 1])
                ins.then_inc(s_ttr, 1)

            def gate_head(l, c, b):
                v = vhead(c, b)
                dsa, h = ATTENDED[v]
                merge = any(other == h for _, other in ATTENDED[:v])
                gates = pj[:, c % 3, :, (128 + 256 * b if dsa else 384):][:, :, 0:P]
                dve.wait_ge(s_exp, l * HEADS + v + 1)
                nc.vector.reciprocal(rinv[:, :], rsum[:, v % 2, :])
                link(nc.vector.tensor_scalar(gates, gates, 0.5, 0.5, ALU.mult, ALU.add))
                dve.wait_ge(s_av, l * HEADS + v + 1)
                cols = slice(h * DH, (h + 1) * DH)
                for t in range(TT):
                    dst = gtmp[:, t, :] if merge else mixed[:, t, cols]
                    ins = nc.vector.scalar_tensor_tensor(out=dst, in0=ps[:, OUT, t * P:(t + 1) * P],
                                                         scalar=rinv[:, t:t + 1], in1=gates[:, t, :],
                                                         op0=ALU.mult, op1=ALU.mult)
                if merge:
                    link(ins)
                    ins = nc.vector.tensor_tensor(mixed[:, :, cols], mixed[:, :, cols], gtmp, ALU.add)
                ins.then_inc(s_gated, 1)
                dve.wait_ge(s_gated, l * HEADS + v + 1)

            def add_index(l, i):
                dve.wait_ge(s_relu, 4 * l + i + 1)
                for b in range(2):
                    for t, cols in enumerate((slice(0, P), slice(P, 3 * P))):
                        first = i == 0 and b == 0
                        ins = nc.vector.scalar_tensor_tensor(
                            out=score[:, cols], in0=relu[:, b, cols], scalar=wis[:, t, 2 * i + b:2 * i + b + 1],
                            in1=causal[:, cols] if first else score[:, cols], op0=ALU.mult, op1=ALU.add)
                    if b == 0:
                        link(ins)
                ins.then_inc(s_iacc, 1)
                dve.wait_ge(s_iacc, 4 * l + i + 1)

            def take_top(last):
                for t, cols in enumerate((slice(0, P), slice(P, 3 * P))):
                    ins = nc.vector.max(max8[:, t, :], score[:, cols])
                link(ins)
                for t, cols in enumerate((slice(0, P), slice(P, 3 * P))):
                    ins = nc.vector.match_replace(score[:, cols], max8[:, t, :], score[:, cols], TAKEN)
                link(ins)
                if last:
                    link(nc.vector.tensor_scalar(keep[:, :], score[:, :], 0.5 * TAKEN, NEG, ALU.is_gt, ALU.mult))
                    link(nc.vector.tensor_tensor(keep[:, :], keep[:, :], causal, ALU.add))

            def act_lo(l, kind, i, dst, src, hi):
                dve.wait_ge(s_act_hi, l * N_TURN + turn_no(kind, i))
                nc.vector.tensor_tensor(dst, src, hi.bitcast(F32), ALU.subtract).then_inc(s_act_lo, 1)

            def h_lo(l, kind, t):
                for i in range(2):
                    at = (slice(None), slice(4 * i, 4 * i + 4), slice(t * P, (t + 1) * P))
                    act_lo(l, kind, 2 * t + i, t_lo[at], ps[:, PTB + i, :].rearrange("p (k n) -> p k n", k=4), t_hi[at])

            def mix_lo(l, i):
                at = (slice(None), i % 2, slice(None), slice(None))
                act_lo(l, "mix", i, m_lo[at], ps[:, QKT, :].rearrange("p (k n) -> p k n", k=2), m_hi[at])

            def m_lo_split(l, j, t):
                at = (slice(None), j % 2, slice(None), slice(t * P, (t + 1) * P))
                act_lo(l, "m", 2 * j + t, m_lo[at], ps[:, PTB + t, 0:256].rearrange("p (k n) -> p k n", k=2), m_hi[at])

            def scaled(t):
                nc.vector.tensor_tensor(hbuf[:, t, :], x[:, t, :], scale_t[:, :], ALU.mult).then_inc(s_dve, 1)
                links[0] += 1
                made[t] = links[0]

            def normed(n, t):
                dve.wait_ge(s_rstd, n + 1)
                dve.wait_ge(s_dve, made[t])
                for i in range(2):
                    cols = slice(512 * i, 512 * i + 512)
                    shift = shift_t[:, cols] if n > 1 else ps[:, QKT + i, :]
                    ins = nc.vector.scalar_tensor_tensor(out=hbuf[:, t, cols], in0=hbuf[:, t, cols],
                                                         scalar=rstd[:, t:t + 1], in1=shift,
                                                         op0=ALU.mult, op1=ALU.add)
                    ins.then_inc(s_h, 1)

            def gated(l, mid, n, t):
                dve.wait_ge(s_sq, n + 1)
                nc.vector.tensor_tensor(hbuf[:, t, :], ps[:, 2 * t:2 * t + 2, :].rearrange("p b n -> p (b n)"),
                                        gate_t[:, :], ALU.mult).then_inc(s_dve, 1)
                links[0] += 1
                made[t] = links[0]

            def added(l, mid, n, t):
                dve.wait_ge(s_rstd, n + 1)
                dve.wait_ge(s_dve, made[t])
                nc.vector.scalar_tensor_tensor(out=x[:, t, :], in0=hbuf[:, t, :], scalar=rstd[:, t:t + 1],
                                               in1=x[:, t, :], op0=ALU.mult, op1=ALU.add).then_inc(s_xup, 1)
                dve.wait_ge(s_xup, 4 * l + (0 if mid else 2) + t + 1)

            made = [0, 0]

            def border(l, mid):
                n = 2 + 8 * l + (0 if mid else 4)
                more = mid or l + 1 < DEPTH
                gated(l, mid, n, 0)
                added(l, mid, n, 0)
                if more:
                    dve.wait_ge(s_table, 2 + 4 * l + (2 if mid else 4))
                    scaled(0)
                gated(l, mid, n + 1, 1)
                added(l, mid, n + 1, 1)
                if more:
                    dve.wait_ge(s_shift, 2 * l + (1 if mid else 2))
                    normed(n + 2, 0)
                    scaled(1)
                    to, kind = (l, "h2") if mid else (l + 1, "h1")
                    h_lo(to, kind, 0)
                    normed(n + 3, 1)
                    h_lo(to, kind, 1)

            nc.vector.memset(ones[:, :], 1.0).then_inc(s_ones, 1)
            dve.wait_ge(s_ones, 1)
            dve.wait_ge(s_cs, 1)
            for k in range(KT):
                ins = nc.vector.tensor_scalar(wide_c[k // 4][:, (k % 4) * P:(k % 4 + 1) * P], ones[:, :],
                                              cs[:, k:k + 1], None, ALU.mult)
            ins.then_inc(s_wide, 1)
            add_pieces(KT)
            dve.wait_ge(s_gain0, 16)
            for half in range(2):
                first_scale(half)
            dve.wait_ge(s_x, 16)
            dve.wait_ge(s_table, 2)
            for t in range(TT):
                scaled(t)
            dve.wait_ge(s_adasum, 3)
            for t in range(TT):
                normed(t, t)
            h_lo(0, "h1", 0)
            for u in range(RAW):
                split_lo(0, u)
            h_lo(0, "h1", 1)

            for l in range(DEPTH):
                for u in range(RAW, RING):
                    split_lo(l, u)
                add_pieces(sum(MIX_PIECES[1]))
                for s in range(2, N_CHUNK + 3):
                    if is_head(s - 2):
                        mask_scores(l, vhead(s - 2))
                    if s == 2:
                        rope(l, 0)
                    if s - 1 < N_CHUNK:
                        rope(l, s - 1)
                    if s in (3, 4):
                        add_index(l, 2 * (s - 3))
                    if is_head(s - 3):
                        gate_head(l, s - 3, 0)
                    for u in SPLITS[s][:-1]:
                        split_lo(l, u)
                    if s in MIX_PIECES:
                        add_pieces(MIX_PIECES[s][0])
                    if s in TOP_STEPS:
                        take_top(False)
                    if is_pair(s - 3):
                        gate_head(l, s - 3, 1)
                    if is_pair(s - 2):
                        mask_scores(l, vhead(s - 2, 1))
                    if s in (3, 4):
                        add_index(l, 2 * (s - 3) + 1)
                    if s in TOP_STEPS:
                        take_top(s == TOP_STEPS[-1])
                    if s == N_CHUNK + 2:
                        mix_lo(l, 3)
                    split_lo(l, SPLITS[s][-1])
                    if N_CHUNK - 1 <= s < N_CHUNK + 2:
                        mix_lo(l, s - N_CHUNK + 1)
                    if s in MIX_PIECES:
                        add_pieces(MIX_PIECES[s][1])
                    if s in MIX_TABLES:
                        make_table(4 * l + MIX_TABLES.index(s) + 1)

                border(l, True)
                for j in range(N_FF):
                    ahead, behind = up_splits(j)
                    if j:
                        m_lo_split(l, j - 1, 1)
                    for u in ahead:
                        split_lo(l, u)
                    for t in range(TT):
                        dve.wait_ge(s_silu, 2 * (l * N_FF + j) + t + 1)
                        if j:
                            dve.wait_ge(s_turn, l * N_TURN + turn_no("m", 2 * (j - 1) + t))
                        nc.vector.tensor_tensor(ffn_m[:, t, :], ffn_s[:, t, :], ps[:, QKT + t, 256:512],
                                                ALU.mult).then_inc(s_m, 1)
                    m_lo_split(l, j, 0)
                    many = ffn_pieces(l)[0][j]
                    split_lo(l, behind[0])
                    add_pieces(min(many, 1))
                    split_lo(l, behind[1])
                    add_pieces(max(many - 1, 0))
                    if j in ffn_pieces(l)[1]:
                        make_table(4 * l + 3 + ffn_pieces(l)[1].index(j))
                m_lo_split(l, N_FF - 1, 1)
                border(l, False)

        @block.tensor
        def _(pe):
            def product(dst, hi, lo, w_h, w_l, first, last):
                nc.tensor.matmul(dst, hi, w_h, start=first, stop=False)
                nc.tensor.matmul(dst, hi, w_l, start=False, stop=False)
                return nc.tensor.matmul(dst, lo, w_h, start=False, stop=last)

            def project(l, c, t, between=None):
                units = chunk_units(c)
                cols = SMALL if c == 0 else 512
                bank = (c % 2) + 2 * t
                if c < 2:
                    if l:
                        pe.wait_ge(s_xup, 4 * l - 1 + t)
                    else:
                        pe.wait_ge(s_table, 2)
                elif c == 2:
                    pe.wait_ge(s_pj, l * N_MM + 1 + 2 * t)
                else:
                    pe.wait_ge(s_pj, l * N_MM + mm_no(c - 2, t))
                per = KT // len(units)
                for k in range(KT):
                    if c == 0 and k % 4 == 0:
                        pe.wait_ge(s_act_lo, l * N_TURN + turn_no("h1", 2 * t + k // 4))
                    U = l * UNITS + units[k // per]
                    if t == 0 and k % per == 0:
                        pe.wait_ge(s_lo, U + 1)
                    a = (k % per) * cols
                    ins = product(ps[:, bank, 0:cols], t_hi[:, k, t * P:(t + 1) * P], t_lo[:, k, t * P:(t + 1) * P],
                                  w_hi[:, U % RING, a:a + cols], w_lo[:, U % RING, a:a + cols], k == 0, k == KT - 1)
                    if t == 1 and k == per - 1 < KT - 1:
                        ins.then_inc(s_used, 1)
                    if between and k == KT // 2 - 1:
                        between()
                ins.then_inc(s_mm, 1)

            def down(l, u, t, hi, lo, first, last, between=None):
                U = l * UNITS + u
                pe.wait_ge(s_lo, U + 1)
                for n in range(2):
                    for k in range(2):
                        a = k * D + n * 512
                        ins = product(ps[:, 2 * t + n, :], hi[:, k, t * P:(t + 1) * P], lo[:, k, t * P:(t + 1) * P],
                                      w_hi[:, U % RING, a:a + 512], w_lo[:, U % RING, a:a + 512],
                                      first and k == 0, last and k == 1)
                    if between and n == 0:
                        between()
                if last:
                    ins.then_inc(s_y, 1)
                elif t == 1:
                    ins.then_inc(s_used, 1)

            def turn(dst, blocks, signal):
                for i, blk in enumerate(blocks):
                    ins = nc.tensor.transpose(dst[:, i * P:(i + 1) * P], blk, ident)
                ins.then_inc(signal, 1)

            def turn_h(l, kind, t):
                for i in range(2):
                    pe.wait_ge(s_h, 8 * l + (0 if kind == "h1" else 4) + 2 * t + i + 1)
                    if t:
                        pe.wait_ge(s_act_lo, l * N_TURN + turn_no(kind, i))
                    turn(ps[:, PTB + i, :], [hbuf[:, t, (4 * i + k) * P:(4 * i + k + 1) * P] for k in range(4)], s_turn)

            def turn_index(l):
                pe.wait_ge(s_roped, l * N_ROPE + 2)
                turn(ps[:, OUT, :], [kid[:, t, :, :].rearrange("p a n -> p (a n)") for t in range(TT)], s_iT)
                for i, bank in enumerate((QKT, PTB)):
                    turn(ps[:, bank, :], [pj[:, 1, t, (2 * i + j) * P:(2 * i + j + 1) * P]
                                          for j in range(2) for t in range(TT)], s_iT)

            def turn_qk(l, c):
                pe.wait_ge(s_roped, l * N_ROPE + c + 1)
                if c == 2:
                    pe.wait_ge(s_iqk, 3 * l + 2)
                else:
                    pe.wait_ge(s_qkT, l * N_QT + c - 2)
                step = 2 if is_pair(c) else 1
                turn(ps[:, QKT, :], [pj[:, c % 3, t, step * j * P:(step * j + 1) * P]
                                     for j in range(2) for t in range(TT)], s_qT)

            def index_logits(l, i):
                pe.wait_ge(s_iqk, 3 * l + 3)
                if i:
                    pe.wait_ge(s_relu, 4 * l + i)
                for b, bank in enumerate((SCO, OUT)):
                    rows = slice(IDH * b, IDH * (b + 1))
                    for t in range(TT):
                        ins = nc.tensor.matmul(ps[:, bank, t * P:(2 * t + 1) * P],
                                               qiT[rows, i, t * P:(t + 1) * P], kiT[rows, 0:(t + 1) * P],
                                               start=True, stop=True)
                ins.then_inc(s_logit, 1)

            def scores(l, c, b):
                v = vhead(c, b)
                n = l * HEADS + v
                dsa, h = ATTENDED[v]
                pe.wait_ge(s_qkT, l * N_QT + c - 1)
                if v == 0:
                    pe.wait_ge(s_relu, 4 * l + 4)
                else:
                    pe.wait_ge(s_ttr, n)
                q = qkT[:, 256 * b:256 * b + SEQ]
                kv = h // (8 // KV_HEADS)
                k = kbT[:, kv * SEQ:(kv + 1) * SEQ] if dsa else qkT[:, SEQ:]
                nc.tensor.matmul(ps[:, SCO, 0:P], q[:, 0:P], k[:, 0:P], start=True, stop=True)
                nc.tensor.matmul(ps[:, SCO, P:3 * P], q[:, P:SEQ], k, start=True, stop=True).then_inc(s_sco, 1)

            def turn_prob(l, v):
                n = l * HEADS + v
                pe.wait_ge(s_exp, n + 1)
                if v:
                    pe.wait_ge(s_pT, n)
                else:
                    pe.wait_ge(s_iqk, 3 * l + 3)
                turn(ps[:, PTB, :], [prob[:, i * P:(i + 1) * P] for i in range(3)], s_prT)

            def weigh_values(l, c, b):
                v = vhead(c, b)
                n = l * HEADS + v
                pe.wait_ge(s_pT, n + 1)
                if n:
                    pe.wait_ge(s_gated, n)
                dsa, h = ATTENDED[v]
                kv = h // (8 // KV_HEADS)
                val = vb[:, :, kv * DH:(kv + 1) * DH] if dsa else pj[:, c % 3, :, 256:384]
                nc.tensor.matmul(ps[:, OUT, 0:P], probT[:, 0:P], val[:, 0, :], start=True, stop=True)
                nc.tensor.matmul(ps[:, OUT, P:2 * P], probT[:, P:2 * P], val[:, 0, :], start=True, stop=False)
                nc.tensor.matmul(ps[:, OUT, P:2 * P], probT[:, 2 * P:3 * P], val[:, 1, :],
                                 start=False, stop=True).then_inc(s_av, 1)

            def first_modulation():
                pe.wait_ge(s_wide, 1)
                for k in range(KT):
                    n = KT + k
                    src, landed, count = piece_at(n)
                    if k == KT - 2:
                        pe.wait_ge(s_adause, KT)
                        for half in range(2):
                            nc.tensor.matmul(ps[:, PTB + half, :], ones[:, :], acc[:, 512 * half:512 * half + 512],
                                             start=True, stop=True).then_inc(s_adasum, 1)
                    pe.wait_ge(landed, count)
                    for half in range(2):
                        ins = nc.tensor.matmul(ps[:, QKT + half, :], wide_c[k // 4][:, (k % 4) * P:(k % 4 + 1) * P],
                                               src[:, 512 * half:512 * half + 512], start=k == 0, stop=False)
                    ins.then_inc(s_fed, 1)
                pe.wait_ge(s_bias0[1], 16)
                for half in range(2):
                    ins = nc.tensor.matmul(ps[:, QKT + half, :], ones[:, :], gate_t[:, 512 * half:512 * half + 512],
                                           start=False, stop=True)
                ins.then_inc(s_adasum, 1)

            def turn_mixed(l, i):
                pe.wait_ge(s_gated, l * HEADS + 1 + max(v for v, (_, h) in enumerate(ATTENDED) if h // 2 == i))
                if i < 2:
                    pe.wait_ge(s_qkT, l * N_QT + N_QT - 1 + i)
                if i:
                    pe.wait_ge(s_act_lo, l * N_TURN + turn_no("mix", i - 1))
                turn(ps[:, QKT, :],
                     [mixed[:, t, (2 * i + k) * P:(2 * i + k + 1) * P] for k in range(2) for t in range(TT)], s_turn)

            def out_unit(l, i, t, between=None):
                pe.wait_ge(s_act_lo, l * N_TURN + turn_no("mix", i))
                if i == 0:
                    pe.wait_ge(s_pj, l * N_MM + mm_no(N_CHUNK - 1, t))
                down(l, OUT_UNIT + i, t, m_hi[:, i % 2], m_lo[:, i % 2], i == 0, i == KT // 2 - 1, between)

            def up(l, j, t):
                n = l * N_FF + j
                if j:
                    pe.wait_ge(s_m, 2 * n - 1 + t)
                for k in range(KT):
                    if j == 0 and k % 4 == 0:
                        pe.wait_ge(s_act_lo, l * N_TURN + turn_no("h2", 2 * t + k // 4))
                    U = l * UNITS + up_unit(j) + k // 4
                    if t == 0 and k % 4 == 0:
                        pe.wait_ge(s_lo, U + 1)
                    a = (k % 4) * 512
                    ins = product(ps[:, QKT + t, :], t_hi[:, k, t * P:(t + 1) * P], t_lo[:, k, t * P:(t + 1) * P],
                                  w_hi[:, U % RING, a:a + 512], w_lo[:, U % RING, a:a + 512], k == 0, k == KT - 1)
                    if t == 1 and k == 3:
                        ins.then_inc(s_used, 1)
                ins.then_inc(s_up, 1)

            def turn_m(l, j, t):
                pe.wait_ge(s_m, 2 * (l * N_FF + j) + t + 1)
                pe.wait_ge(s_act_lo, l * N_TURN + (turn_no("m", 2 * (j - 1) + t) if j else turn_no("h2", 2 + t)))
                turn(ps[:, PTB + t, :], [ffn_m[:, t, k * P:(k + 1) * P] for k in range(2)], s_turn)

            def down_chunk(l, j, t):
                pe.wait_ge(s_act_lo, l * N_TURN + turn_no("m", 2 * j + 1))
                if j == 0:
                    pe.wait_ge(s_xup, 4 * l + 1 + t)
                down(l, down_unit(j), t, m_hi[:, j % 2], m_lo[:, j % 2], j == 0, j == N_FF - 1)

            first_modulation()
            pe.wait_ge(s_const, 32)

            for l in range(DEPTH):
                turn_h(l, "h1", 0)
                project(l, 0, 0)
                project(l, 1, 0)
                turn_h(l, "h1", 1)
                project(l, 0, 1)
                project(l, 1, 1)
                for s in range(2, N_CHUNK + 3):
                    if s < N_CHUNK:
                        project(l, s, 0)
                    else:
                        out_unit(l, s - N_CHUNK, 0)
                    if s == 2:
                        turn_index(l)
                    elif s - 1 < N_CHUNK:
                        turn_qk(l, s - 1)
                    if is_pair(s - 3):
                        weigh_values(l, s - 3, 1)
                    if is_head(s - 2):
                        turn_prob(l, vhead(s - 2))
                    if is_pair(s - 2):
                        scores(l, s - 2, 1)
                    if s in (3, 4):
                        index_logits(l, 2 * (s - 3) + 1)
                    mixed_turn = None
                    if N_CHUNK - 1 <= s < N_CHUNK + 2:
                        mixed_turn = lambda: turn_mixed(l, s - N_CHUNK + 1)
                    elif s == N_CHUNK + 2:
                        turn_mixed(l, KT // 2 - 1)
                    if s < N_CHUNK:
                        project(l, s, 1, mixed_turn)
                    else:
                        out_unit(l, s - N_CHUNK, 1, mixed_turn)
                    if is_head(s - 1):
                        scores(l, s - 1, 0)
                    if is_head(s - 2):
                        weigh_values(l, s - 2, 0)
                    if is_pair(s - 2):
                        turn_prob(l, vhead(s - 2, 1))
                    if s in (2, 3):
                        index_logits(l, 2 * (s - 2))
                for t in range(TT):
                    out_unit(l, KT // 2 - 1, t)

                for t in range(TT):
                    turn_h(l, "h2", t)
                    up(l, 0, t)
                turn_m(l, 0, 0)
                for j in range(1, N_FF):
                    up(l, j, 0)
                    turn_m(l, j - 1, 1)
                    up(l, j, 1)
                    turn_m(l, j, 0)
                    if j < N_FF - 1:
                        for t in range(TT):
                            down_chunk(l, j - 1, t)
                down_chunk(l, N_FF - 2, 0)
                turn_m(l, N_FF - 1, 1)
                down_chunk(l, N_FF - 1, 0)
                down_chunk(l, N_FF - 2, 1)
                down_chunk(l, N_FF - 1, 1)


_INS = ("x_in", "c_in", "pos_in", "const_in", "w_ada", "b_ada", "gains", "w_stream")


def laid_out(x, c, positions, w_ada, b_ada, g_pre_mix, g_post_mix, w_in, w_out, g_pre_ffn, g_post_ffn,
             w_gate, w_up, w_down):
    f = lambda a: np.asarray(a)
    w_in, w_out, w_gate, w_up, w_down = map(f, (w_in, w_out, w_gate, w_up, w_down))
    sizes = (D, D, D, D, KV_HEADS * DH, KV_HEADS * DH, IH * IDH, IDH, IH, D, D)
    qa, ka, va, qb, kb, vb, qi, ki, wi, ga, gb, end = np.concatenate([[0], np.cumsum(sizes)])
    head = lambda base, h: list(range(base + h * DH, base + (h + 1) * DH))
    chunks = [list(range(ki, wi + IH)), list(range(qi, qi + IH * IDH)), list(range(kb, kb + 512))]
    chunks += [head(qb, h) + head(gb, h) + head(qb, h + 1) + head(gb, h + 1) if dsa
               else head(qa, h) + head(ka, h) + head(va, h) + head(ga, h) for dsa, h in HEAD_CHUNKS]
    stream = np.zeros((DEPTH, UNITS, P, UNIT), np.float32)
    for l in range(DEPTH):
        def put(u, rows):
            k = rows.shape[0] // P
            flat = rows.reshape(k, P, -1).transpose(1, 0, 2).reshape(P, -1)
            stream[l, u, :, :flat.shape[1]] = flat

        put(0, w_in[l][:, chunks[0]])
        for n in range(1, N_CHUNK):
            for i, u in enumerate(chunk_units(n)):
                put(u, w_in[l][i * 512:(i + 1) * 512, chunks[n]])
        for i in range(KT // 2):
            put(OUT_UNIT + i, w_out[l][256 * i:256 * i + 256])
        for j in range(N_FF):
            both = np.concatenate([w_gate[l][:, 256 * j:256 * j + 256], w_up[l][:, 256 * j:256 * j + 256]], axis=1)
            for i in range(2):
                put(up_unit(j) + i, both[i * 512:(i + 1) * 512])
            put(down_unit(j), w_down[l][256 * j:256 * j + 256])
    const = np.zeros((P, N_CONST), np.float32)
    const[:, 0:P] = np.eye(P)
    past = np.arange(P)[None, :] <= np.arange(P)[:, None]
    const[:, P:2 * P] = np.where(past, 0.0, NEG)
    const[:, 3 * P:4 * P] = np.where(past, 0.0, NEG)
    const[:, 4 * P:] = (THETA ** (-np.arange(HALF) / HALF)).astype(np.float32)
    return {
        "x_in": f(x).reshape(TT, P, D).transpose(1, 0, 2),
        "c_in": f(c).reshape(KT, P).T,
        "pos_in": f(positions).reshape(TT, P).T,
        "const_in": const,
        "w_ada": f(w_ada),
        "b_ada": f(b_ada),
        "gains": np.stack([f(g_pre_mix), f(g_post_mix), f(g_pre_ffn), f(g_post_ffn)]),
        "w_stream": stream,
    }


def kernel(**inputs):
    import concourse.bacc as bacc
    from concourse.bass_utils import run_bass_kernel_spmd

    nc = bacc.Bacc("TRN2", target_bir_lowering=False, num_devices=1)
    arrays = {k: np.ascontiguousarray(v) for k, v in laid_out(**inputs).items()}
    args = [nc.dram_tensor(n, arrays[n].shape, mybir.dt.from_np(arrays[n].dtype), kind="ExternalInput").ap() for n in _INS]
    out = nc.dram_tensor("out", (TT, P, D), F32, kind="ExternalOutput").ap()
    hybrid_decoder_trunk(nc, *args, out)
    r = run_bass_kernel_spmd(nc, [arrays], core_ids=[0])
    return r.results[0]["out"].reshape(1, SEQ, D)
```

```python
from contextlib import ExitStack

import numpy as np

import concourse.bass as bass
from concourse import mybir

P = 128
D = 1024
SEQ = 256
DEPTH = 2
TT = SEQ // P
KT = D // P
DH = 128
HALF = DH // 4 // 2
IH, IDH = 8, 64
IHALF = IDH // 4 // 2
FF = 2816
N_TOP = SEQ // 4
THETA = 500000.0
EPS = 1e-6
NEG = -1e30
TAKEN = -3e38
SCALE = DH ** -0.5
KV_HEADS = 2

UNIT = 2048
SMALL = IDH + IH
N_CHUNK = 15
FIRST_HEAD = 3
HEAD_CHUNKS = ([(False, h) for h in range(4)] + [(True, 0), (False, 4), (True, 2), (False, 5)]
               + [(True, 4), (False, 6), (True, 6), (False, 7)])
N_FF = FF // 256
OUT_UNIT = 1 + 2 * (N_CHUNK - 1)
FFN_UNIT = OUT_UNIT + KT // 2
UNITS = FFN_UNIT + 3 * N_FF
RAW, RING = 3, 5
PIECE = 1024
PARTS = 6
ADA_RING = 2
START = 2 * KT
START_ORDER = (8, 0, 9, 1, 10, 2, 11, 3, 4, 12, 5, 13, 6, 7, 14, 15)
PRO_OTHER = START - 2 * ADA_RING
N_CONST = P + 3 * P + HALF

F32 = mybir.dt.float32
F32R = mybir.dt.float32r
I32 = mybir.dt.int32
ALU = mybir.AluOpType
ACT = mybir.ActivationFunctionType

SH1, SC1, GT1, SH2, SC2, GT2 = range(6)


def up_unit(j):
    return FFN_UNIT + (3 * j - 1 if j else 0)


def down_unit(j):
    return FFN_UNIT + (3 * j + 4 if j < N_FF - 1 else 3 * j + 2)


def chunk_units(c):
    return [0] if c == 0 else [2 * c - 1, 2 * c]


def two_pi_parts():
    rest, parts = 2 * np.pi, []
    for low in (9, 21, 33, 45):
        part = np.floor(rest * 2.0 ** low) / 2.0 ** low
        parts.append(float(part))
        rest -= part
    return parts


RSQRT_BITS = float(0x5F3759DF - 2 ** 22 - 2 ** 31)
NEWTON = 3
ROUND = 1.5 * 2.0 ** 23
PI_IN = 3.1415925

SPLITS = {2: [u + RING for u in (0, 1, 2)]} | {s: [u + RING for u in chunk_units(s - 1)] for s in range(3, N_CHUNK + 1)} \
    | {N_CHUNK + 1: [OUT_UNIT + RING], N_CHUNK + 2: [OUT_UNIT + 1 + RING]}

MADE = [(0, SC1), (0, SH1)] + [p for l in range(DEPTH) for p in (
    (l, GT1), (l, SC2), (l, SH2), (l, GT2), (l + 1, SC1), (l + 1, SH1))][:PARTS * DEPTH - 2]
MIX_PIECES = {1: (2, 0)} | {s: (1, 1) for s in (2, 3, 4)} | {s: (1, 0) for s in (5, 6, 7)} \
    | {s: (1, 1) for s in range(8, 14)} | {14: (1, 0)}
MIX_TABLES = (5, 11)
TOP_STEPS = range(5, 5 + N_TOP // 16)


def ffn_pieces(l):
    if l + 1 < DEPTH:
        return (2, 3, 3, 2, 3, 2, 3, 2, 2, 2, 0), (4, 8)
    return (1, 1, 1, 1, 1, 1, 1, 1, 0, 0, 0), (9,)


def up_splits(j):
    ahead = [OUT_UNIT + 2 + RING, OUT_UNIT + 3 + RING] if j == 0 else [down_unit(j - 2) + RING] if j > 1 else []
    return ahead, [up_unit(j) + RING, up_unit(j) + 1 + RING]


START_FILL = (5, 5, 18, 11, 0, 8, 0, 4)
MIXER_FILL, FFN_FILL, TURN_FILL = 16, 23, 4
TURN_AT = 7

NORMS = [(-1, False, "x", t) for t in range(TT)] + [n for l in range(DEPTH) for n in (
    (l, mid, of, t) for mid in (True, False) for t in range(TT) for of in ("yx" if mid or l + 1 < DEPTH else "y"))]


OWN_NORMS = [n for n, (l, _, of, t) in enumerate(NORMS) if l >= 0 and of == "x"]
POOL_NORMS = [n for n in range(len(NORMS)) if n not in OWN_NORMS]


def last_norm(n):
    return max((m for m in range(n) if NORMS[m][3] == NORMS[n][3]), default=None)


ATTENDED = [(dsa, h + b) for dsa, h in HEAD_CHUNKS for b in range(1 + dsa)]
HEADS = len(ATTENDED)


def hybrid_decoder_trunk(nc, x_in, c_in, pos_in, const_in, w_ada, b_ada, gains, w_stream, out):
    with ExitStack() as ctx:
        def sb(name, shape, dt=F32):
            return ctx.enter_context(nc.sbuf_tensor(name, shape, dt))

        def sem(name):
            return ctx.enter_context(nc.semaphore(name))

        ps = ctx.enter_context(nc.psum_tensor("ps", [P, 8, 512], F32))
        QKT, SCO, PTB, OUT = 4, 5, 6, 7

        raw = sb("raw", [P, RAW, UNIT])
        w_hi = sb("w_hi", [P, RING, UNIT], F32R)
        w_lo = sb("w_lo", [P, RING, UNIT], F32R)
        ada = sb("ada", [P, ADA_RING, PIECE])

        x = sb("x", [P, TT, D])
        t_hi = sb("t_hi", [P, KT, SEQ], F32R)
        t_lo = sb("t_lo", [P, KT, SEQ], F32R)
        mixed = sb("mixed", [P, TT, D])
        scale_t = sb("scale_t", [P, D])
        shift_t = sb("shift_t", [P, D])
        gate_t = sb("gate_t", [P, D])
        acc = sb("acc", [P, D])
        tables = (gate_t, scale_t, shift_t)

        pj = sb("pj", [P, 3, TT, 512])
        hbuf = pj[:, :, :, :].rearrange("p b t n -> p b (t n)")
        junk = hbuf[:, 2, :]
        kiw = sb("kiw", [P, TT, SMALL])
        kid = sb("kid", [P, TT, 2, IDH])
        kiT = sb("kiT", [P, SEQ])
        region = sb("region", [P, 4 * SEQ])
        qiT = region[:, :].rearrange("p (b n) -> p b n", b=4)
        sx = region[:, 0:3 * P]
        prob = region[:, 3 * P:6 * P]
        qkT = sb("qkT", [P, 512])
        kbT = sb("kbT", [P, 512])
        wide_c = (qkT, kbT)
        vb = sb("vb", [P, TT, 256])
        relu = sb("relu", [P, 2, 3 * P])
        probT = relu[:, 0, :]
        ffn_s = relu[:, :, 0:256]
        score = sb("score", [P, 3 * P])
        keep = sb("keep", [P, 3 * P])
        ffn_m = sb("ffn_m", [P, TT, 256])
        m_hi = sb("m_hi", [P, 2, 2, SEQ], F32R)
        m_lo = sb("m_lo", [P, 2, 2, SEQ], F32R)
        rope_a, rope_b = ffn_m[:, 0, :], ffn_m[:, 1, :]

        const = sb("const", [P, N_CONST])
        ident = const[:, 0:P]
        causal = const[:, P:4 * P]
        inv_freq = const[:, 4 * P:4 * P + HALF]
        ones = sb("ones", [P, P])
        pos = sb("pos", [P, TT], I32)
        cT = sb("cT", [P, KT])
        cs = sb("cs", [P, KT])
        posf = sb("posf", [P, TT])
        ang = sb("ang", [P, 7, TT, HALF])
        cos_t = sb("cos_t", [P, TT, 2 * HALF])
        sin_t = sb("sin_t", [P, TT, 2 * HALF])
        icos_t = sb("icos_t", [P, TT, 2 * IHALF])
        isin_t = sb("isin_t", [P, TT, 2 * IHALF])
        wis = sb("wis", [P, TT, IH])
        gtmp = kiT[:, :].rearrange("p (t n) -> p t n", t=TT)
        max8 = sb("max8", [P, 2, 8])
        ssq = sb("ssq", [P, TT])
        rstd = sb("rstd", [P, TT])
        rms = sb("rms", [P, TT, 2])
        nmax = sb("nmax", [P, 2, TT])
        rsum = sb("rsum", [P, 2, TT])
        rinv = sb("rinv", [P, TT])

        s_c = sem("c_landed")
        s_const = sem("const_landed")
        s_x = sem("x_landed")
        s_raw = [sem(f"raw_landed{i}") for i in range(RAW)]
        s_ada = [sem(f"ada_landed{i}") for i in range(ADA_RING)]
        s_bias = [sem(f"bias_landed{i}") for i in range(3)]
        s_bias0 = [sem(f"first_bias_landed{i}") for i in range(2)]
        s_gain0 = sem("first_gain_landed")
        s_gain = sem("gain_landed")
        s_pro = [sem(f"start_piece_landed{i}") for i in range(PRO_OTHER)]
        s_out = sem("out_stored")
        s_zero = sem("sum_zeroed")
        s_shift = sem("shift_table")
        s_reduced = sem("modulation_reduced")
        s_ang = sem("angles")
        s_rope_t = sem("rotary_tables")
        s_pool = sem("pool_chain")
        s_rstd = sem("rstd_ready")
        s_own_rstd = sem("own_rstd_ready")
        s_cs = sem("silu_c")
        s_sin = sem("sines")
        s_hi = sem("hi_split")
        s_pj = sem("pj_copied")
        s_iqk = sem("index_qk_copied")
        s_qkT = sem("qkT_copied")
        s_relu = sem("logits_rectified")
        s_exp = sem("exp_done")
        s_pT = sem("probT_copied")
        s_act_hi = sem("act_hi_split")
        s_sq = sem("squares_summed")
        s_silu = sem("silu_done")
        s_lo = sem("lo_split")
        s_roped = sem("roped")
        s_iacc = sem("index_summed")
        s_ttr = sem("masked_min")
        s_gated = sem("head_gated")
        s_act_lo = sem("act_lo_split")
        s_h = sem("h_ready")
        s_xup = sem("x_updated")
        s_final = sem("half_result_ready")
        s_m = sem("m_ready")
        s_adause = sem("ada_used")
        s_table = sem("table_made")
        s_dve = sem("dve_chain")
        s_ones = sem("ones_set")
        s_wide = sem("wide_c_made")
        s_mm = sem("projected")
        s_used = sem("unit_used")
        s_iT = sem("index_turned")
        s_qT = sem("qk_turned")
        s_logit = sem("index_logits")
        s_sco = sem("scores")
        s_prT = sem("prob_turned")
        s_av = sem("head_out")
        s_turn = sem("act_turned")
        s_y = sem("sublayer_out")
        s_up = sem("up_projected")
        s_adasum = sem("modulation_summed")
        s_fed = sem("shift_piece_used")

        N_MM, N_ROPE, N_QT, N_TURN, N_SPLIT = 2 * N_CHUNK, N_CHUNK, N_CHUNK - 2, 14, 12 + 2 * N_FF

        start_at = ([ada[:, i, :] for i in range(ADA_RING)] + [mixed[:, t, :] for t in range(TT)]
                    + [hbuf[:, i, :] for i in range(3)] + [region[:, :]]
                    + [raw[:, i // 2, (i % 2) * PIECE:(i % 2 + 1) * PIECE] for i in range(2 * RAW)])

        def piece_at(n):
            if n < ADA_RING:
                return start_at[n], s_ada[n], 16
            if n < START - ADA_RING:
                return start_at[n], s_pro[n - ADA_RING], 16
            return ada[:, n % ADA_RING, :], s_ada[n % ADA_RING], 16 * (2 + (n - START + ADA_RING) // ADA_RING)

        def mm_no(c, t):
            return 2 * t + c + 1 if c < 2 else 2 * c + t + 1

        def turn_no(kind, i):
            return {"h1": 0, "mix": 4, "h2": 8, "m": 12}[kind] + i + 1

        def is_head(c):
            return FIRST_HEAD <= c < N_CHUNK

        def is_pair(c):
            return is_head(c) and HEAD_CHUNKS[c - FIRST_HEAD][0]

        def vhead(c, b=0):
            dsa, h = HEAD_CHUNKS[c - FIRST_HEAD]
            return ATTENDED.index((dsa, h + b))

        def last_head(c):
            return vhead(c, 1 if is_pair(c) else 0)

        used_units = ([chunk_units(c)[0] for c in range(1, N_CHUNK)] + [OUT_UNIT + i for i in range(KT // 2 - 1)]
                      + sorted([up_unit(j) for j in range(N_FF)] + [down_unit(j) for j in range(N_FF - 1)]))
        N_USED = len(used_units)

        def inverse_rms(engine, link, t, done):
            u, y, e = rms[:, t, 0:1], rstd[:, t:t + 1], rms[:, t, 1:2]
            link(engine.tensor_scalar(u, ssq[:, t:t + 1], EPS, 0.5, ALU.add, ALU.mult))
            link(engine.tensor_scalar(y.bitcast(I32), u.bitcast(I32), -0.5, RSQRT_BITS, ALU.mult, ALU.add))
            for step in range(NEWTON):
                link(engine.tensor_scalar(e, y, u, y, ALU.mult, ALU.mult))
                ins = engine.tensor_scalar(y, e, 1.5, y, ALU.subtract, ALU.mult)
                if step < NEWTON - 1:
                    link(ins)
            ins.then_inc(done, 1)

        def wait_rstd(eng, n):
            if n in OWN_NORMS:
                eng.wait_ge(s_own_rstd, OWN_NORMS.index(n) + 1)
            else:
                eng.wait_ge(s_rstd, POOL_NORMS.index(n) + 1)

        def wait_multiplied(eng, U):
            l, u = U // UNITS, U % UNITS
            if u in used_units:
                eng.wait_ge(s_used, l * N_USED + used_units.index(u) + 1)
            elif u < OUT_UNIT:
                eng.wait_ge(s_mm, l * N_MM + mm_no(u // 2, 1))
            elif u == FFN_UNIT - 1:
                eng.wait_ge(s_y, 4 * l + 2)
            elif u == UNITS - 1:
                eng.wait_ge(s_y, 4 * l + 4)
            else:
                j = [up_unit(j) + 1 for j in range(N_FF)].index(u)
                eng.wait_ge(s_up, 2 * (l * N_FF + j) + 2)

        block = ctx.enter_context(nc.Block())

        @block.sync
        def _(sp):
            pieces = [0]

            def load_unit(l, u):
                U = l * UNITS + u
                if U >= DEPTH * UNITS:
                    return
                if U >= RAW:
                    sp.wait_ge(s_lo, U - RAW + 1)
                n = KT * SMALL if U % UNITS == 0 else UNIT
                sp.dma_start(raw[:, U % RAW, 0:n], w_stream[U // UNITS, U % UNITS, :, 0:n]).then_inc(s_raw[U % RAW], 16)

            def load_pieces(count):
                for _ in range(count):
                    n = START_ORDER[pieces[0]] if pieces[0] < START else pieces[0]
                    l, part = MADE[n // KT]
                    dst, landed, _ = piece_at(n)
                    if n >= START + ADA_RING:
                        sp.wait_ge(s_adause, n - KT - ADA_RING + 1)
                    elif n >= START:
                        sp.wait_ge(s_fed, n - KT - ADA_RING + 1)
                    elif n >= START - ADA_RING:
                        sp.wait_ge(s_adause, n - START + ADA_RING + 1)
                    k = n % KT
                    sp.dma_start(dst, w_ada[l, k * P:(k + 1) * P, part * D:(part + 1) * D]).then_inc(landed, 16)
                    pieces[0] += 1

            sp.dma_start(cT[:], c_in).then_inc(s_c, 16)
            load_pieces(2)
            sp.dma_start(const[:], const_in).then_inc(s_const, 16)
            sp.dma_start(pos[:], pos_in).then_inc(s_const, 16)
            load_pieces(4)
            sp.dma_start(x[:, :, :], x_in).then_inc(s_x, 16)
            load_pieces(10)
            for u in range(RAW):
                sp.wait_ge(s_fed, 2 * u + 2)
                load_unit(0, u)
            for l in range(DEPTH):
                for u in range(RAW, RING):
                    load_unit(l, u)
                load_pieces(sum(MIX_PIECES[1]))
                for s in range(2, N_CHUNK + 3):
                    for half in range(2):
                        for u in SPLITS[s][:-1] if half == 0 else SPLITS[s][-1:]:
                            load_unit(l, u)
                        if s in MIX_PIECES:
                            load_pieces(MIX_PIECES[s][half])
                for j in range(N_FF):
                    ahead, behind = up_splits(j)
                    many = ffn_pieces(l)[0][j]
                    for u in ahead:
                        load_unit(l, u)
                    load_pieces(max(many - 2, 0))
                    load_unit(l, behind[0])
                    load_pieces(min(many, 1))
                    load_unit(l, behind[1])
                    load_pieces(many > 1)
            for t in range(TT):
                for i in range(2):
                    sp.wait_ge(s_final, 2 * t + i + 1)
                    sp.dma_start(out[t, :, 512 * i:512 * i + 512],
                                 x[:, t, 512 * i:512 * i + 512]).then_inc(s_out, 16)
            sp.wait_ge(s_out, 2 * 16 * TT)

        @block.gpsimd
        def _(pool):
            links = [0]

            def link(ins):
                ins.then_inc(s_pool, 1)
                links[0] += 1
                pool.wait_ge(s_pool, links[0])

            zeroed = [0]

            def seed(buf, l, part, landed):
                nc.gpsimd.memset(buf[:, :], 0.0).then_inc(s_zero, 1)
                zeroed[0] += 1
                pool.wait_ge(s_zero, zeroed[0])
                pool.dma_start(buf[0:1, :], b_ada[l:l + 1, part * D:(part + 1) * D]).then_inc(landed, 16)

            def reduce(n, i):
                pool.wait_ge(s_adause, KT * n)
                nc.gpsimd.partition_all_reduce(acc[:, :], tables[i][:, :], P, bass.bass_isa.ReduceOp.add).then_inc(s_reduced, 1)
                pool.wait_ge(s_reduced, n - 1)

            def finish(n, i, l, which):
                reduce(n, i)
                pool.dma_start(tables[i][:, :], gains[which, l:l + 1, :].broadcast_to([P, D])).then_inc(s_gain, 16)

            def finish_shift(n, done):
                reduce(n, 2)
                nc.gpsimd.tensor_copy(shift_t[:, :], acc[:, :]).then_inc(s_shift, 1)
                pool.wait_ge(s_shift, done)

            def wait_norm_used(n):
                l, mid, of, t = NORMS[n]
                if of == "y":
                    pool.wait_ge(s_xup, 4 * l + (0 if mid else 2) + t + 1)
                else:
                    pool.wait_ge(s_h, 8 * l + (4 if mid else 8) + 2 * t + 2)

            def norm(n):
                if n in OWN_NORMS:
                    return
                t = NORMS[n][3]
                pool.wait_ge(s_sq, n + 1)
                if n > 1:
                    wait_norm_used(last_norm(n))
                inverse_rms(nc.gpsimd, link, t, s_rstd)

            seed(acc, 0, SC1, s_bias0[0])
            seed(gate_t, 0, SH1, s_bias0[1])
            pool.dma_start(scale_t[:, :], gains[0, 0:1, :].broadcast_to([P, D])).then_inc(s_gain0, 16)

            pool.wait_ge(s_const, 32)
            link(nc.gpsimd.tensor_copy(posf[:, :], pos[:, :]))
            th, turns, r, quarter, high, low, part = (ang[:, i] for i in range(7))
            for t in range(TT):
                ins = nc.gpsimd.tensor_scalar(th[:, t, :], inv_freq, posf[:, t:t + 1], None, ALU.mult)
            link(ins)
            link(nc.gpsimd.tensor_scalar(turns, th, 1.0 / (2 * np.pi), ROUND, ALU.mult, ALU.add))
            link(nc.gpsimd.tensor_scalar(turns, turns, -ROUND, None, ALU.add))
            link(nc.gpsimd.tensor_scalar(high, turns, ROUND * 2.0 ** 11, None, ALU.add))
            link(nc.gpsimd.tensor_scalar(high, high, -ROUND * 2.0 ** 11, None, ALU.add))
            link(nc.gpsimd.tensor_tensor(low, turns, high, ALU.subtract))
            parts = two_pi_parts()
            for which, i in ((high, 0), (low, 0), (high, 1), (low, 1), (high, 2), (low, 2), (high, 3)):
                link(nc.gpsimd.tensor_scalar(part, which, parts[i], None, ALU.mult))
                link(nc.gpsimd.tensor_tensor(r, th if which is high and i == 0 else r, part, ALU.subtract))
            link(nc.gpsimd.tensor_scalar(r, r, PI_IN, -PI_IN, ALU.min, ALU.max))
            link(nc.gpsimd.tensor_scalar(quarter, r, np.pi / 2, None, ALU.add))
            link(nc.gpsimd.tensor_scalar(turns, quarter, np.pi, -2 * np.pi, ALU.is_gt, ALU.mult))
            link(nc.gpsimd.tensor_tensor(quarter, quarter, turns, ALU.add))
            nc.gpsimd.tensor_scalar(quarter, quarter, PI_IN, -PI_IN, ALU.min, ALU.max).then_inc(s_ang, 1)
            for t in range(TT):
                norm(t)
            pool.wait_ge(s_sin, 1)
            sine, cosine = ang[:, 4], ang[:, 5]
            for w, c_t, s_t, step in ((HALF, cos_t, sin_t, 1), (IHALF, icos_t, isin_t, HALF // IHALF)):
                for i in range(2):
                    nc.gpsimd.tensor_copy(c_t[:, :, i * w:(i + 1) * w], cosine[:, :, ::step])
                nc.gpsimd.tensor_copy(s_t[:, :, 0:w], sine[:, :, ::step])
                ins = nc.gpsimd.tensor_scalar(s_t[:, :, w:], sine[:, :, ::step], -1.0, None, ALU.mult)
            ins.then_inc(s_rope_t, 1)

            pool.wait_ge(s_fed, KT)
            for l in range(DEPTH):
                n = 2 + l * PARTS
                if l:
                    pool.wait_ge(s_xup, 4 * l)
                seed(gate_t, l, GT1, s_bias[0])
                pool.wait_ge(s_h, 8 * l + 4)
                seed(scale_t, l, SC2, s_bias[1])
                seed(shift_t, l, SH2, s_bias[2])
                finish(n, 0, l, 1)
                pool.wait_ge(s_table, 2 + 4 * l + 1)
                finish(n + 1, 1, l, 2)
                pool.wait_ge(s_table, 2 + 4 * l + 2)
                finish_shift(n + 2, 2 * l + 1)
                for i in range(2 + 8 * l, 6 + 8 * l):
                    norm(i)
                more = l + 1 < DEPTH
                pool.wait_ge(s_xup, 4 * l + 2)
                seed(gate_t, l, GT2, s_bias[0])
                if more:
                    pool.wait_ge(s_h, 8 * l + 8)
                    seed(scale_t, l + 1, SC1, s_bias[1])
                    seed(shift_t, l + 1, SH1, s_bias[2])
                finish(n + 3, 0, l, 3)
                if more:
                    pool.wait_ge(s_table, 2 + 4 * l + 3)
                    finish(n + 4, 1, l + 1, 0)
                    pool.wait_ge(s_table, 2 + 4 * l + 4)
                    finish_shift(n + 5, 2 * l + 2)
                for i in range(6 + 8 * l, min(10 + 8 * l, len(NORMS))):
                    norm(i)

        @block.scalar
        def _(act):
            def split_hi(l, u):
                U = l * UNITS + u
                if U >= DEPTH * UNITS:
                    return
                n = KT * SMALL if U % UNITS == 0 else UNIT
                act.wait_ge(s_raw[U % RAW], 16 * (U // RAW + 1))
                if U >= RING:
                    wait_multiplied(act, U - RING)
                nc.scalar.activation(w_hi[:, U % RING, 0:n], raw[:, U % RAW, 0:n], ACT.Copy).then_inc(s_hi, 1)

            def copy_chunk(l, c, t):
                act.wait_ge(s_mm, l * N_MM + mm_no(c, t))
                src = ps[:, (c % 2) + 2 * t, :]
                if c == 0:
                    nc.scalar.activation(kiw[:, t, :], src[:, 0:SMALL], ACT.Copy).then_inc(s_pj, 1)
                    return
                dst = pj[:, c % 3, t, :]
                if c == 1:
                    act.wait_ge(s_turn, l * N_TURN + turn_no("h1", 3))
                elif c == 4:
                    act.wait_ge(s_iT, l * 3 + 3)
                elif c == 5:
                    act.wait_ge(s_qT, l * N_QT + 1)
                elif c > 5:
                    act.wait_ge(s_gated, l * HEADS + last_head(c - 3) + 1)
                if c == 1:
                    nc.scalar.activation(dst, src, ACT.Copy).then_inc(s_pj, 1)
                elif c == 2:
                    nc.scalar.activation(dst[:, 0:256], src[:, 0:256], ACT.Copy)
                    nc.scalar.activation(vb[:, t, :], src[:, 256:512], ACT.Copy).then_inc(s_pj, 1)
                elif not is_pair(c):
                    nc.scalar.activation(dst[:, 0:384], src[:, 0:384], ACT.Copy)
                    nc.scalar.activation(dst[:, 384:512], src[:, 384:512], ACT.Tanh, scale=0.5).then_inc(s_pj, 1)
                else:
                    d = dst.rearrange("p (h a n) -> p h a n", h=2, a=2)
                    q = src.rearrange("p (h a n) -> p h a n", h=2, a=2)
                    nc.scalar.activation(d[:, :, 0, :], q[:, :, 0, :], ACT.Copy)
                    nc.scalar.activation(d[:, :, 1, :], q[:, :, 1, :], ACT.Tanh, scale=0.5).then_inc(s_pj, 1)

            def softmax_exp(l, v):
                n = l * HEADS + v
                act.wait_ge(s_ttr, n + 1)
                if n:
                    act.wait_ge(s_prT, n)
                if n > 1:
                    act.wait_ge(s_gated, n - 1)
                nc.scalar.activation(prob[:, 0:P], sx[:, 0:P], ACT.Exp, bias=nmax[:, v % 2, 0:1], scale=-1.0,
                                     accum_out=rsum[:, v % 2, 0:1])
                nc.scalar.activation(prob[:, P:3 * P], sx[:, P:3 * P], ACT.Exp, bias=nmax[:, v % 2, 1:2], scale=-1.0,
                                     accum_out=rsum[:, v % 2, 1:2]).then_inc(s_exp, 1)

            def copy_probT(l, v):
                act.wait_ge(s_prT, l * HEADS + v + 1)
                if v:
                    act.wait_ge(s_av, l * HEADS + v)
                else:
                    act.wait_ge(s_iacc, 4 * l + 4)
                nc.scalar.activation(probT, ps[:, PTB, 0:3 * P], ACT.Copy).then_inc(s_pT, 1)

            def copy_qkT(l, c):
                act.wait_ge(s_qT, l * N_QT + c - 1)
                if c == 2:
                    nc.scalar.activation(kbT[:, :], ps[:, QKT, :], ACT.Copy).then_inc(s_qkT, 1)
                    return
                if c > FIRST_HEAD:
                    act.wait_ge(s_sco, l * HEADS + last_head(c - 1) + 1)
                nc.scalar.activation(qkT[:, :], ps[:, QKT, :], ACT.Copy).then_inc(s_qkT, 1)

            def copy_index(l):
                act.wait_ge(s_iT, l * 3 + 1)
                nc.scalar.activation(kiT[:, :], ps[:, OUT, 0:SEQ], ACT.Copy).then_inc(s_iqk, 1)
                for i, bank in enumerate((QKT, PTB)):
                    act.wait_ge(s_iT, l * 3 + 2 + i)
                    nc.scalar.activation(region[:, 512 * i:512 * i + 512], ps[:, bank, :], ACT.Copy).then_inc(s_iqk, 1)

            def rectify(l, i):
                act.wait_ge(s_logit, 4 * l + i + 1)
                if i:
                    act.wait_ge(s_iacc, 4 * l + i)
                for b, bank in enumerate((SCO, OUT)):
                    ins = nc.scalar.activation(relu[:, b, :], ps[:, bank, 0:3 * P], ACT.Relu, scale=float(IDH) ** -0.5)
                ins.then_inc(s_relu, 1)

            def act_hi(l, kind, i, dst, src):
                act.wait_ge(s_turn, l * N_TURN + turn_no(kind, i))
                nc.scalar.activation(dst, src, ACT.Copy).then_inc(s_act_hi, 1)

            def h_hi(l, kind, t):
                for i in range(2):
                    act_hi(l, kind, 2 * t + i, t_hi[:, 4 * i:4 * i + 4, t * P:(t + 1) * P],
                           ps[:, PTB + i, :].rearrange("p (k n) -> p k n", k=4))

            def mix_hi(l, i):
                act_hi(l, "mix", i, m_hi[:, i % 2, :, :], ps[:, QKT, :].rearrange("p (k n) -> p k n", k=2))

            def m_hi_split(l, j, t):
                if j:
                    act.wait_ge(s_m, 2 * (l * N_FF + j) + t + 1)
                    if j > 1:
                        wait_multiplied(act, l * UNITS + down_unit(j - 2))
                    nc.scalar.activation(m_hi[:, j % 2, t, :], ffn_m[:, t, :], ACT.Copy).then_inc(s_act_hi, 1)
                    return
                act_hi(l, "m", 2 * j + t, m_hi[:, j % 2, :, t * P:(t + 1) * P],
                       ps[:, PTB + t, 0:256].rearrange("p (k n) -> p k n", k=2))

            def sum_squares(n):
                l, mid, of, t = NORMS[n]
                count = 4 * l + (0 if mid else 2) + t + 1
                if of == "y":
                    act.wait_ge(s_y, count)
                elif l < 0:
                    act.wait_ge(s_x, 16)
                else:
                    act.wait_ge(s_xup, count)
                if n > 1:
                    wait_rstd(act, last_norm(n))
                if n:
                    act.wait_ge(s_sq, n)
                src = x[:, t, :] if of == "x" else ps[:, 2 * t:2 * t + 2, :].rearrange("p b n -> p (b n)")
                dst = junk if l >= 0 else ps[:, 0:2, :].rearrange("p b n -> p (b n)")
                nc.scalar.activation(dst, src, ACT.Square, scale=float(D) ** -0.5,
                                     accum_out=ssq[:, t:t + 1]).then_inc(s_sq, 1)

            def border(l, mid):
                to, kind = (l, "h2") if mid else (l + 1, "h1")
                own = [n for n, norm in enumerate(NORMS) if norm[:2] == (l, mid)]
                for n in own:
                    if l >= 0 and NORMS[n][2:] == ("x", 1):
                        h_hi(to, kind, 0)
                    sum_squares(n)
                if l >= 0 and to < DEPTH:
                    h_hi(to, kind, 1)

            act.wait_ge(s_c, 16)
            nc.scalar.activation(cs[:, :], cT[:, :], ACT.Silu).then_inc(s_cs, 1)
            act.wait_ge(s_ang, 1)
            nc.scalar.activation(ang[:, 4:6], ang[:, 2:4], ACT.Sin).then_inc(s_sin, 1)
            border(-1, False)
            for u in range(RAW - 1):
                split_hi(0, u)
            h_hi(0, "h1", 0)
            split_hi(0, RAW - 1)
            h_hi(0, "h1", 1)

            for l in range(DEPTH):
                copy_chunk(l, 0, 0)
                for u in range(RAW, RING):
                    split_hi(l, u)
                copy_chunk(l, 1, 0)
                for s in range(2, N_CHUNK + 3):
                    if s == 2:
                        copy_chunk(l, 0, 1)
                    if s - 1 < N_CHUNK:
                        copy_chunk(l, s - 1, 1)
                    if is_pair(s - 3):
                        copy_probT(l, vhead(s - 3, 1))
                    for u in SPLITS[s][:-1]:
                        split_hi(l, u)
                    if is_head(s - 2):
                        softmax_exp(l, vhead(s - 2))
                    if s in (3, 4):
                        rectify(l, 2 * (s - 3))
                    if s == 2:
                        copy_index(l)
                    elif s - 1 < N_CHUNK:
                        copy_qkT(l, s - 1)
                    if is_head(s - 2):
                        copy_probT(l, vhead(s - 2))
                    if s < N_CHUNK:
                        split_hi(l, SPLITS[s][-1])
                    if s >= N_CHUNK - 1:
                        mix_hi(l, s - N_CHUNK + 1)
                    if is_pair(s - 2):
                        softmax_exp(l, vhead(s - 2, 1))
                    if s >= N_CHUNK:
                        split_hi(l, SPLITS[s][-1])
                    if s in (3, 4):
                        rectify(l, 2 * (s - 3) + 1)
                    if s < N_CHUNK:
                        copy_chunk(l, s, 0)

                border(l, True)
                for j in range(N_FF):
                    ahead, behind = up_splits(j)
                    for u in ahead[:1]:
                        split_hi(l, u)
                    if j == 1:
                        m_hi_split(l, 0, 1)
                    for t in range(TT):
                        if t:
                            if j:
                                m_hi_split(l, j, 0)
                            for u in ahead[1:]:
                                split_hi(l, u)
                        act.wait_ge(s_up, 2 * (l * N_FF + j) + t + 1)
                        n = l * N_FF + j
                        if n:
                            act.wait_ge(s_m, 2 * n + t - 1)
                        nc.scalar.activation(ffn_s[:, t, :], ps[:, QKT + t, 0:256], ACT.Silu).then_inc(s_silu, 1)
                    m_hi_split(l, j, 1 if j else 0)
                    for u in behind:
                        split_hi(l, u)
                border(l, False)

        @block.vector
        def _(dve):
            links = [0]

            def link(ins):
                ins.then_inc(s_dve, 1)
                links[0] += 1
                dve.wait_ge(s_dve, links[0])

            def split_lo(l, u):
                U = l * UNITS + u
                if U >= DEPTH * UNITS:
                    return
                n = KT * SMALL if U % UNITS == 0 else UNIT
                dve.wait_ge(s_hi, U + 1)
                nc.vector.tensor_tensor(w_lo[:, U % RING, 0:n], raw[:, U % RAW, 0:n],
                                        w_hi[:, U % RING, 0:n].bitcast(F32), ALU.subtract).then_inc(s_lo, 1)

            pieces = [0]

            def add_pieces(many):
                for _ in range(many):
                    m = pieces[0]
                    n = m if m < KT else m + KT
                    k, part = n % KT, n // KT
                    buf = tables[(part - 2) % 3] if part else acc
                    if k == 0:
                        dve.wait_ge(s_bias[(part - 2) % 3] if part else s_bias0[0], 16 * ((part - 2) // 3 + 1) if part else 16)
                    src, landed, count = piece_at(n)
                    dve.wait_ge(landed, count)
                    if m:
                        dve.wait_ge(s_adause, m)
                    nc.vector.scalar_tensor_tensor(out=buf[:, :], in0=src, scalar=cs[:, k:k + 1],
                                                   in1=buf[:, :], op0=ALU.mult, op1=ALU.add).then_inc(s_adause, 1)
                    pieces[0] += 1

            def first_scale(half):
                cols = slice(512 * half, 512 * half + 512)
                dve.wait_ge(s_adasum, half + 1)
                nc.vector.scalar_tensor_tensor(out=scale_t[:, cols], in0=ps[:, PTB + half, :], scalar=1.0,
                                               in1=scale_t[:, cols], op0=ALU.add, op1=ALU.mult).then_inc(s_table, 1)

            def make_table(n):
                table, extra = ((gate_t, 0.0), (scale_t, 1.0))[(n - 1) % 2]
                dve.wait_ge(s_gain, 16 * n)
                nc.vector.scalar_tensor_tensor(out=table[:, :], in0=acc[:, :], scalar=extra, in1=table[:, :],
                                               op0=ALU.add, op1=ALU.mult).then_inc(s_table, 1)

            def rotate(src, dst, heads, width, cos, sin, done):
                half = width // 2
                a = rope_a[:, 0:TT * heads * width].rearrange("p (t h w) -> p t h w", t=TT, h=heads)
                b = rope_b[:, 0:TT * heads * width].rearrange("p (t h w) -> p t h w", t=TT, h=heads)
                for t in range(TT):
                    cb = cos[:, t:t + 1, :].broadcast_to([P, heads, width])
                    sn = sin[:, t:t + 1, :].broadcast_to([P, heads, width])
                    nc.vector.tensor_tensor(a[:, t], src[:, t], cb, ALU.mult)
                    ins = nc.vector.tensor_tensor(b[:, t], src[:, t], sn, ALU.mult)
                link(ins)
                for t in range(TT):
                    x1, x2 = dst[t]
                    h = x1.shape[1]
                    a1 = a[:, t] if h == heads else a[:, t].broadcast_to([P, h, width])
                    b1 = b[:, t] if h == heads else b[:, t].broadcast_to([P, h, width])
                    nc.vector.tensor_tensor(x1, a1[:, :, 0:half], b1[:, :, half:], ALU.add)
                    ins = nc.vector.tensor_tensor(x2, a1[:, :, half:], b1[:, :, 0:half], ALU.add)
                ins.then_inc(s_roped, 1)
                dve.wait_ge(s_roped, done)

            def rope(l, c):
                done = l * N_ROPE + c + 1
                if c == 0 and l == 0:
                    dve.wait_ge(s_rope_t, 1)
                dve.wait_ge(s_pj, l * N_MM + (3 if c == 0 else 2 * c + 2))
                if c == 0:
                    nc.vector.tensor_scalar(wis[:, :, :], kiw[:, :, IDH:], float(IH) ** -0.5, None, ALU.mult)
                    nc.vector.tensor_copy(kid[:, :, 0, :], kiw[:, :, 0:IDH])
                    link(nc.vector.tensor_copy(kid[:, :, 1, :], kiw[:, :, 0:IDH]))
                    src = kiw[:, :, 0:2 * IHALF].rearrange("p t (h w) -> p t h w", h=1)
                    dst = [(kid[:, t, :, 0:IHALF], kid[:, t, :, IHALF:2 * IHALF]) for t in range(TT)]
                    rotate(src, dst, 1, 2 * IHALF, icos_t, isin_t, done)
                    return
                b = pj[:, c % 3, :, :]
                if c == 1:
                    v = b.rearrange("p t (h w) -> p t h w", h=IH)
                    rotate(v[:, :, :, 0:2 * IHALF],
                           [(v[:, t, :, 0:IHALF], v[:, t, :, IHALF:2 * IHALF]) for t in range(TT)],
                           IH, 2 * IHALF, icos_t, isin_t, done)
                    return
                v = b.rearrange("p t (h w) -> p t h w", h=2 if is_pair(c) else 4)[:, :, 0:2, :]
                rotate(v[:, :, :, 0:2 * HALF],
                       [(v[:, t, :, 0:HALF], v[:, t, :, HALF:2 * HALF]) for t in range(TT)],
                       2, 2 * HALF, cos_t, sin_t, done)

            def mask_scores(l, v):
                n = l * HEADS + v
                dve.wait_ge(s_sco, n + 1)
                if n:
                    dve.wait_ge(s_exp, n)
                m = keep if ATTENDED[v][0] else causal
                for t, cols in enumerate((slice(0, P), slice(P, 3 * P))):
                    ins = nc.vector.tensor_tensor_reduce(sx[:, cols], ps[:, SCO, cols], m[:, cols], -SCALE, 3e38,
                                                         ALU.add, ALU.min, nmax[:, v % 2, t:t + 1])
                ins.then_inc(s_ttr, 1)

            def gate_head(l, c, b):
                v = vhead(c, b)
                dsa, h = ATTENDED[v]
                merge = any(other == h for _, other in ATTENDED[:v])
                gates = pj[:, c % 3, :, (128 + 256 * b if dsa else 384):][:, :, 0:P]
                dve.wait_ge(s_exp, l * HEADS + v + 1)
                nc.vector.reciprocal(rinv[:, :], rsum[:, v % 2, :])
                link(nc.vector.tensor_scalar(gates, gates, 0.5, 0.5, ALU.mult, ALU.add))
                dve.wait_ge(s_av, l * HEADS + v + 1)
                cols = slice(h * DH, (h + 1) * DH)
                for t in range(TT):
                    dst = gtmp[:, t, :] if merge else mixed[:, t, cols]
                    ins = nc.vector.scalar_tensor_tensor(out=dst, in0=ps[:, OUT, t * P:(t + 1) * P],
                                                         scalar=rinv[:, t:t + 1], in1=gates[:, t, :],
                                                         op0=ALU.mult, op1=ALU.mult)
                if merge:
                    link(ins)
                    ins = nc.vector.tensor_tensor(mixed[:, :, cols], mixed[:, :, cols], gtmp, ALU.add)
                ins.then_inc(s_gated, 1)
                dve.wait_ge(s_gated, l * HEADS + v + 1)

            def add_index(l, i):
                dve.wait_ge(s_relu, 4 * l + i + 1)
                for b in range(2):
                    for t, cols in enumerate((slice(0, P), slice(P, 3 * P))):
                        first = i == 0 and b == 0
                        ins = nc.vector.scalar_tensor_tensor(
                            out=score[:, cols], in0=relu[:, b, cols], scalar=wis[:, t, 2 * i + b:2 * i + b + 1],
                            in1=causal[:, cols] if first else score[:, cols], op0=ALU.mult, op1=ALU.add)
                    if b == 0:
                        link(ins)
                ins.then_inc(s_iacc, 1)
                dve.wait_ge(s_iacc, 4 * l + i + 1)

            def take_top(last):
                for t, cols in enumerate((slice(0, P), slice(P, 3 * P))):
                    ins = nc.vector.max(max8[:, t, :], score[:, cols])
                link(ins)
                for t, cols in enumerate((slice(0, P), slice(P, 3 * P))):
                    ins = nc.vector.match_replace(score[:, cols], max8[:, t, :], score[:, cols], TAKEN)
                link(ins)
                if last:
                    link(nc.vector.tensor_scalar(keep[:, :], score[:, :], 0.5 * TAKEN, NEG, ALU.is_gt, ALU.mult))
                    link(nc.vector.tensor_tensor(keep[:, :], keep[:, :], causal, ALU.add))

            def act_lo(l, kind, i, dst, src, hi):
                dve.wait_ge(s_act_hi, l * N_SPLIT + turn_no(kind, i))
                nc.vector.tensor_tensor(dst, src, hi.bitcast(F32), ALU.subtract).then_inc(s_act_lo, 1)

            def h_lo(l, kind, t):
                for i in range(2):
                    at = (slice(None), slice(4 * i, 4 * i + 4), slice(t * P, (t + 1) * P))
                    act_lo(l, kind, 2 * t + i, t_lo[at], ps[:, PTB + i, :].rearrange("p (k n) -> p k n", k=4), t_hi[at])

            def mix_lo(l, i):
                at = (slice(None), i % 2, slice(None), slice(None))
                act_lo(l, "mix", i, m_lo[at], ps[:, QKT, :].rearrange("p (k n) -> p k n", k=2), m_hi[at])

            def m_lo_split(l, j, t):
                if j:
                    act_lo(l, "m", 2 * j + t, m_lo[:, j % 2, t, :], ffn_m[:, t, :], m_hi[:, j % 2, t, :])
                    return
                at = (slice(None), j % 2, slice(None), slice(t * P, (t + 1) * P))
                act_lo(l, "m", 2 * j + t, m_lo[at], ps[:, PTB + t, 0:256].rearrange("p (k n) -> p k n", k=2), m_hi[at])

            def scaled(t):
                nc.vector.tensor_tensor(hbuf[:, t, :], x[:, t, :], scale_t[:, :], ALU.mult).then_inc(s_dve, 1)
                links[0] += 1
                made[t] = links[0]

            def normed(l, mid, t):
                n = NORMS.index((l, mid, "x", t))
                if n in OWN_NORMS:
                    dve.wait_ge(s_sq, n + 1)
                    inverse_rms(nc.vector, link, t, s_own_rstd)
                wait_rstd(dve, n)
                dve.wait_ge(s_dve, made[t])
                for i in range(2):
                    cols = slice(512 * i, 512 * i + 512)
                    shift = shift_t[:, cols] if l >= 0 else ps[:, QKT + i, :]
                    nc.vector.scalar_tensor_tensor(out=hbuf[:, t, cols], in0=hbuf[:, t, cols],
                                                   scalar=rstd[:, t:t + 1], in1=shift,
                                                   op0=ALU.mult, op1=ALU.add).then_inc(s_h, 1)

            def gated(l, mid, t):
                dve.wait_ge(s_sq, NORMS.index((l, mid, "y", t)) + 1)
                nc.vector.tensor_tensor(hbuf[:, t, :], ps[:, 2 * t:2 * t + 2, :].rearrange("p b n -> p (b n)"),
                                        gate_t[:, :], ALU.mult).then_inc(s_dve, 1)
                links[0] += 1
                made[t] = links[0]

            def added(l, mid, t):
                wait_rstd(dve, NORMS.index((l, mid, "y", t)))
                dve.wait_ge(s_dve, made[t])
                if not mid and l + 1 == DEPTH:
                    for i in range(2):
                        cols = slice(512 * i, 512 * i + 512)
                        nc.vector.scalar_tensor_tensor(out=x[:, t, cols], in0=hbuf[:, t, cols], scalar=rstd[:, t:t + 1],
                                                       in1=x[:, t, cols], op0=ALU.mult, op1=ALU.add).then_inc(s_final, 1)
                    return
                nc.vector.scalar_tensor_tensor(out=x[:, t, :], in0=hbuf[:, t, :], scalar=rstd[:, t:t + 1],
                                               in1=x[:, t, :], op0=ALU.mult, op1=ALU.add).then_inc(s_xup, 1)
                dve.wait_ge(s_xup, 4 * l + (0 if mid else 2) + t + 1)

            made = [0, 0]

            def border(l, mid):
                to, kind = (l, "h2") if mid else (l + 1, "h1")
                more = to < DEPTH
                gated(l, mid, 0)
                added(l, mid, 0)
                if more:
                    dve.wait_ge(s_table, 2 + 4 * l + (2 if mid else 4))
                    scaled(0)
                    dve.wait_ge(s_shift, 2 * l + (1 if mid else 2))
                    normed(l, mid, 0)
                gated(l, mid, 1)
                if more:
                    h_lo(to, kind, 0)
                added(l, mid, 1)
                if more:
                    scaled(1)
                    normed(l, mid, 1)
                    h_lo(to, kind, 1)

            nc.vector.memset(ones[:, :], 1.0).then_inc(s_ones, 1)
            dve.wait_ge(s_ones, 1)
            dve.wait_ge(s_cs, 1)
            for k in range(KT):
                ins = nc.vector.tensor_scalar(wide_c[k // 4][:, (k % 4) * P:(k % 4 + 1) * P], ones[:, :],
                                              cs[:, k:k + 1], None, ALU.mult)
            ins.then_inc(s_wide, 1)
            add_pieces(KT)
            dve.wait_ge(s_gain0, 16)
            for half in range(2):
                first_scale(half)
            dve.wait_ge(s_x, 16)
            dve.wait_ge(s_table, 2)
            for t in range(TT):
                scaled(t)
            dve.wait_ge(s_fed, KT)
            normed(-1, False, 0)
            split_lo(0, 0)
            split_lo(0, 1)
            h_lo(0, "h1", 0)
            normed(-1, False, 1)
            split_lo(0, 2)
            h_lo(0, "h1", 1)

            for l in range(DEPTH):
                for u in range(RAW, RING):
                    split_lo(l, u)
                add_pieces(sum(MIX_PIECES[1]))
                for s in range(2, N_CHUNK + 1):
                    if is_head(s - 2):
                        mask_scores(l, vhead(s - 2))
                    if s == 2:
                        rope(l, 0)
                    if s - 1 < N_CHUNK:
                        rope(l, s - 1)
                    if s in (3, 4):
                        add_index(l, 2 * (s - 3))
                    if is_head(s - 3):
                        gate_head(l, s - 3, 0)
                    for u in SPLITS[s][:-1]:
                        split_lo(l, u)
                    if s in MIX_PIECES:
                        add_pieces(MIX_PIECES[s][0])
                    if s in TOP_STEPS:
                        take_top(False)
                    if is_pair(s - 3):
                        gate_head(l, s - 3, 1)
                    if is_pair(s - 2):
                        mask_scores(l, vhead(s - 2, 1))
                    if s in (3, 4):
                        add_index(l, 2 * (s - 3) + 1)
                    if s in TOP_STEPS:
                        take_top(s == TOP_STEPS[-1])
                    if s < N_CHUNK:
                        split_lo(l, SPLITS[s][-1])
                    if s >= N_CHUNK - 1:
                        mix_lo(l, s - N_CHUNK + 1)
                    if s in MIX_PIECES:
                        add_pieces(MIX_PIECES[s][1])
                    if s in MIX_TABLES:
                        make_table(4 * l + MIX_TABLES.index(s) + 1)
                c = N_CHUNK - 1
                mask_scores(l, vhead(c))
                gate_head(l, c - 1, 0)
                gate_head(l, c - 1, 1)
                split_lo(l, SPLITS[N_CHUNK][-1])
                mix_lo(l, 2)
                gate_head(l, c, 0)
                mix_lo(l, 3)
                split_lo(l, SPLITS[N_CHUNK + 1][0])
                split_lo(l, SPLITS[N_CHUNK + 2][0])

                border(l, True)
                for j in range(N_FF):
                    ahead, behind = up_splits(j)
                    many = ffn_pieces(l)[0][j]
                    for u in ahead[:1]:
                        split_lo(l, u)
                    add_pieces(max(many - 2, 0))
                    if j == 1:
                        m_lo_split(l, 0, 1)
                    for t in range(TT):
                        if t:
                            if j:
                                m_lo_split(l, j, 0)
                            for u in ahead[1:]:
                                split_lo(l, u)
                        dve.wait_ge(s_silu, 2 * (l * N_FF + j) + t + 1)
                        if j == 1:
                            dve.wait_ge(s_turn, l * N_TURN + turn_no("m", t))
                        elif j:
                            dve.wait_ge(s_act_hi, l * N_SPLIT + turn_no("m", 2 * (j - 1) + t))
                        nc.vector.tensor_tensor(ffn_m[:, t, :], ffn_s[:, t, :], ps[:, QKT + t, 256:512],
                                                ALU.mult).then_inc(s_m, 1)
                    m_lo_split(l, j, 1 if j else 0)
                    split_lo(l, behind[0])
                    add_pieces(min(many, 1))
                    split_lo(l, behind[1])
                    add_pieces(many > 1)
                    if j in ffn_pieces(l)[1]:
                        make_table(4 * l + 3 + ffn_pieces(l)[1].index(j))
                border(l, False)

        @block.tensor
        def _(pe):
            def product(dst, hi, lo, w_h, w_l, first, last):
                nc.tensor.matmul(dst, hi, w_h, start=first, stop=False)
                nc.tensor.matmul(dst, hi, w_l, start=False, stop=False)
                return nc.tensor.matmul(dst, lo, w_h, start=False, stop=last)

            def project(l, c, t, between=None):
                units = chunk_units(c)
                cols = SMALL if c == 0 else 512
                bank = (c % 2) + 2 * t
                if c < 2:
                    if l:
                        pe.wait_ge(s_xup, 4 * l - 1 + t)
                    else:
                        pe.wait_ge(s_table, 2)
                elif c == 2:
                    pe.wait_ge(s_pj, l * N_MM + 1 + 2 * t)
                else:
                    pe.wait_ge(s_pj, l * N_MM + mm_no(c - 2, t))
                per = KT // len(units)
                for k in range(KT):
                    if c == 0 and k % 4 == 0:
                        pe.wait_ge(s_act_lo, l * N_SPLIT + turn_no("h1", 2 * t + k // 4))
                    U = l * UNITS + units[k // per]
                    if t == 0 and k % per == 0:
                        pe.wait_ge(s_lo, U + 1)
                    a = (k % per) * cols
                    ins = product(ps[:, bank, 0:cols], t_hi[:, k, t * P:(t + 1) * P], t_lo[:, k, t * P:(t + 1) * P],
                                  w_hi[:, U % RING, a:a + cols], w_lo[:, U % RING, a:a + cols], k == 0, k == KT - 1)
                    if t == 1 and k == per - 1 < KT - 1:
                        ins.then_inc(s_used, 1)
                    if between and k == KT // 2 - 1:
                        between()
                ins.then_inc(s_mm, 1)

            def down(l, u, t, hi, lo, first, last, between=None):
                U = l * UNITS + u
                pe.wait_ge(s_lo, U + 1)
                for n in range(2):
                    for k in range(2):
                        a = k * D + n * 512
                        ins = product(ps[:, 2 * t + n, :], hi[:, k, t * P:(t + 1) * P], lo[:, k, t * P:(t + 1) * P],
                                      w_hi[:, U % RING, a:a + 512], w_lo[:, U % RING, a:a + 512],
                                      first and k == 0, last and k == 1)
                    if between and n == 0:
                        between()
                if last:
                    ins.then_inc(s_y, 1)
                elif t == 1:
                    ins.then_inc(s_used, 1)

            def turn(dst, blocks, signal):
                for i, blk in enumerate(blocks):
                    ins = nc.tensor.transpose(dst[:, i * P:(i + 1) * P], blk, ident)
                ins.then_inc(signal, 1)

            def turn_h(l, kind, t):
                for i in range(2):
                    pe.wait_ge(s_h, 8 * l + (0 if kind == "h1" else 4) + 2 * t + i + 1)
                    if t:
                        pe.wait_ge(s_act_lo, l * N_SPLIT + turn_no(kind, i))
                    turn(ps[:, PTB + i, :], [hbuf[:, t, (4 * i + k) * P:(4 * i + k + 1) * P] for k in range(4)], s_turn)

            def turn_index(l):
                pe.wait_ge(s_roped, l * N_ROPE + 2)
                turn(ps[:, OUT, :], [kid[:, t, :, :].rearrange("p a n -> p (a n)") for t in range(TT)], s_iT)
                for i, bank in enumerate((QKT, PTB)):
                    turn(ps[:, bank, :], [pj[:, 1, t, (2 * i + j) * P:(2 * i + j + 1) * P]
                                          for j in range(2) for t in range(TT)], s_iT)

            def turn_qk(l, c):
                pe.wait_ge(s_roped, l * N_ROPE + c + 1)
                if c == 2:
                    pe.wait_ge(s_iqk, 3 * l + 2)
                else:
                    pe.wait_ge(s_qkT, l * N_QT + c - 2)
                step = 2 if is_pair(c) else 1
                turn(ps[:, QKT, :], [pj[:, c % 3, t, step * j * P:(step * j + 1) * P]
                                     for j in range(2) for t in range(TT)], s_qT)

            def index_logits(l, i):
                pe.wait_ge(s_iqk, 3 * l + 3)
                if i:
                    pe.wait_ge(s_relu, 4 * l + i)
                for b, bank in enumerate((SCO, OUT)):
                    rows = slice(IDH * b, IDH * (b + 1))
                    for t in range(TT):
                        ins = nc.tensor.matmul(ps[:, bank, t * P:(2 * t + 1) * P],
                                               qiT[rows, i, t * P:(t + 1) * P], kiT[rows, 0:(t + 1) * P],
                                               start=True, stop=True)
                ins.then_inc(s_logit, 1)

            def scores(l, c, b):
                v = vhead(c, b)
                n = l * HEADS + v
                dsa, h = ATTENDED[v]
                pe.wait_ge(s_qkT, l * N_QT + c - 1)
                if v == 0:
                    pe.wait_ge(s_relu, 4 * l + 4)
                else:
                    pe.wait_ge(s_ttr, n)
                q = qkT[:, 256 * b:256 * b + SEQ]
                kv = h // (8 // KV_HEADS)
                k = kbT[:, kv * SEQ:(kv + 1) * SEQ] if dsa else qkT[:, SEQ:]
                nc.tensor.matmul(ps[:, SCO, 0:P], q[:, 0:P], k[:, 0:P], start=True, stop=True)
                nc.tensor.matmul(ps[:, SCO, P:3 * P], q[:, P:SEQ], k, start=True, stop=True).then_inc(s_sco, 1)

            def turn_prob(l, v):
                n = l * HEADS + v
                pe.wait_ge(s_exp, n + 1)
                if v:
                    pe.wait_ge(s_pT, n)
                else:
                    pe.wait_ge(s_iqk, 3 * l + 3)
                turn(ps[:, PTB, :], [prob[:, i * P:(i + 1) * P] for i in range(3)], s_prT)

            def weigh_values(l, c, b):
                v = vhead(c, b)
                n = l * HEADS + v
                pe.wait_ge(s_pT, n + 1)
                if n:
                    pe.wait_ge(s_gated, n)
                dsa, h = ATTENDED[v]
                kv = h // (8 // KV_HEADS)
                val = vb[:, :, kv * DH:(kv + 1) * DH] if dsa else pj[:, c % 3, :, 256:384]
                nc.tensor.matmul(ps[:, OUT, 0:P], probT[:, 0:P], val[:, 0, :], start=True, stop=True)
                nc.tensor.matmul(ps[:, OUT, P:2 * P], probT[:, P:2 * P], val[:, 0, :], start=True, stop=False)
                nc.tensor.matmul(ps[:, OUT, P:2 * P], probT[:, 2 * P:3 * P], val[:, 1, :],
                                 start=False, stop=True).then_inc(s_av, 1)

            def fill(bank, stationary, moving, cols, count):
                for _ in range(count):
                    nc.tensor.matmul(ps[:, bank, 0:cols], stationary, moving, start=True, stop=True)

            def first_modulation():
                pe.wait_ge(s_wide, 1)
                for k in range(KT):
                    n = KT + k
                    src, landed, count = piece_at(n)
                    if k == 4:
                        pe.wait_ge(s_bias0[1], 16)
                        for half in range(2):
                            nc.tensor.matmul(ps[:, QKT + half, :], ones[:, :], gate_t[:, 512 * half:512 * half + 512],
                                             start=False, stop=False)
                    if k == KT - 2:
                        pe.wait_ge(s_adause, KT)
                        for half in range(2):
                            nc.tensor.matmul(ps[:, PTB + half, :], ones[:, :], acc[:, 512 * half:512 * half + 512],
                                             start=True, stop=True).then_inc(s_adasum, 1)
                    pe.wait_ge(landed, count)
                    for half in range(2):
                        ins = nc.tensor.matmul(ps[:, QKT + half, :], wide_c[k // 4][:, (k % 4) * P:(k % 4 + 1) * P],
                                               src[:, 512 * half:512 * half + 512], start=k == 0, stop=k == KT - 1)
                    ins.then_inc(s_fed, 1)
                    fill(2, ones[:, :], ones[:, :], P, START_FILL[k])

            def turn_mixed(l, i):
                pe.wait_ge(s_gated, l * HEADS + 1 + max(v for v, (_, h) in enumerate(ATTENDED) if h // 2 == i))
                if i < 2:
                    pe.wait_ge(s_qkT, l * N_QT + N_QT - 1 + i)
                if i:
                    pe.wait_ge(s_act_lo, l * N_SPLIT + turn_no("mix", i - 1))
                turn(ps[:, QKT, :],
                     [mixed[:, t, (2 * i + k) * P:(2 * i + k + 1) * P] for k in range(2) for t in range(TT)], s_turn)

            def out_unit(l, i, t, between=None):
                pe.wait_ge(s_act_lo, l * N_SPLIT + turn_no("mix", i))
                if i == 0:
                    pe.wait_ge(s_pj, l * N_MM + mm_no(N_CHUNK - 1, t))
                down(l, OUT_UNIT + i, t, m_hi[:, i % 2], m_lo[:, i % 2], i == 0, i == KT // 2 - 1, between)

            def first_up(l, t, between=None):
                for k in range(KT):
                    if k % 4 == 0:
                        pe.wait_ge(s_act_lo, l * N_SPLIT + turn_no("h2", 2 * t + k // 4))
                    U = l * UNITS + up_unit(0) + k // 4
                    if t == 0 and k % 4 == 0:
                        pe.wait_ge(s_lo, U + 1)
                    a = (k % 4) * 512
                    ins = product(ps[:, QKT + t, :], t_hi[:, k, t * P:(t + 1) * P], t_lo[:, k, t * P:(t + 1) * P],
                                  w_hi[:, U % RING, a:a + 512], w_lo[:, U % RING, a:a + 512], k == 0, k == KT - 1)
                    if t == 1 and k == 3:
                        ins.then_inc(s_used, 1)
                    if between and k == TURN_AT:
                        between()
                ins.then_inc(s_up, 1)

            def up_turned(l, j, f):
                pe.wait_ge(s_m, 2 * (l * N_FF + j) - 1 + f)
                for which in range(2):
                    for k in range(KT):
                        U = l * UNITS + up_unit(j) + k // 4
                        if f == which == 0 and k % 4 == 0:
                            pe.wait_ge(s_lo, U + 1)
                        a = (k % 4) * 512 + which * 256 + f * P
                        ins = product(ps[:, QKT + f, which * SEQ:(which + 1) * SEQ],
                                      w_hi[:, U % RING, a:a + P], w_lo[:, U % RING, a:a + P],
                                      t_hi[:, k, :], t_lo[:, k, :], k == 0, k == KT - 1)
                        if f == which == 1 and k == 3:
                            ins.then_inc(s_used, 1)
                ins.then_inc(s_up, 1)

            def turn_m(l, t):
                pe.wait_ge(s_m, 2 * l * N_FF + t + 1)
                pe.wait_ge(s_act_lo, l * N_SPLIT + turn_no("h2", 2 + t))
                turn(ps[:, PTB + t, :], [ffn_m[:, t, k * P:(k + 1) * P] for k in range(2)], s_turn)

            def down_chunk(l, j, t):
                pe.wait_ge(s_act_lo, l * N_SPLIT + turn_no("m", 2 * j + (1 if j else t)))
                if j == 0:
                    pe.wait_ge(s_xup, 4 * l + 1 + t)
                down(l, down_unit(j), t, m_hi[:, j % 2], m_lo[:, j % 2], j == 0, j == N_FF - 1)

            first_modulation()
            pe.wait_ge(s_const, 32)

            for l in range(DEPTH):
                if l:
                    fill(SCO, t_hi[:, 0, 0:P], t_hi[:, 0:2, :], 2 * SEQ, FFN_FILL)
                turn_h(l, "h1", 0)
                if l:
                    fill(SCO, m_hi[:, 0, 0, 0:P], m_hi[:, 0, :, :], 2 * SEQ, TURN_FILL)
                else:
                    fill(2, ones[:, :], ones[:, :], P, 14)
                project(l, 0, 0)
                project(l, 1, 0, lambda: turn_h(l, "h1", 1))
                project(l, 0, 1)
                project(l, 1, 1)
                for s in range(2, N_CHUNK + 2):
                    if s < N_CHUNK:
                        project(l, s, 0)
                    else:
                        out_unit(l, s - N_CHUNK, 0)
                    if s == 2:
                        turn_index(l)
                    elif s - 1 < N_CHUNK:
                        turn_qk(l, s - 1)
                    if is_pair(s - 3):
                        weigh_values(l, s - 3, 1)
                    if is_head(s - 2):
                        turn_prob(l, vhead(s - 2))
                    if is_pair(s - 2):
                        scores(l, s - 2, 1)
                    if s in (3, 4):
                        index_logits(l, 2 * (s - 3) + 1)
                    if s < N_CHUNK - 1:
                        project(l, s, 1)
                    elif s == N_CHUNK - 1:
                        project(l, s, 1, lambda: turn_mixed(l, 0))
                    elif s == N_CHUNK:
                        out_unit(l, 0, 1, lambda: turn_mixed(l, 1))
                    else:
                        out_unit(l, 1, 1, lambda: (weigh_values(l, s - 2, 0), turn_mixed(l, 2)))
                        break
                    if is_head(s - 1):
                        scores(l, s - 1, 0)
                    if is_head(s - 2):
                        weigh_values(l, s - 2, 0)
                    if is_pair(s - 2):
                        turn_prob(l, vhead(s - 2, 1))
                    if s in (2, 3):
                        index_logits(l, 2 * (s - 2))
                out_unit(l, 2, 0, lambda: turn_mixed(l, 3))
                out_unit(l, 3, 0)
                out_unit(l, 2, 1)
                out_unit(l, 3, 1)
                fill(SCO, t_hi[:, 0, 0:P], t_hi[:, 0:2, :], 2 * SEQ, MIXER_FILL)
                turn_h(l, "h2", 0)
                fill(SCO, m_hi[:, 0, 0, 0:P], m_hi[:, 0, :, :], 2 * SEQ, TURN_FILL)
                first_up(l, 0, lambda: turn_h(l, "h2", 1))
                first_up(l, 1)
                turn_m(l, 0)
                for j in range(1, N_FF):
                    up_turned(l, j, 0)
                    if j == 1:
                        turn_m(l, 1)
                    up_turned(l, j, 1)
                    if j < N_FF - 1:
                        for t in range(TT):
                            down_chunk(l, j - 1, t)
                for t in range(TT):
                    for j in (N_FF - 2, N_FF - 1):
                        down_chunk(l, j, t)


_INS = ("x_in", "c_in", "pos_in", "const_in", "w_ada", "b_ada", "gains", "w_stream")


def laid_out(x, c, positions, w_ada, b_ada, g_pre_mix, g_post_mix, w_in, w_out, g_pre_ffn, g_post_ffn,
             w_gate, w_up, w_down):
    f = lambda a: np.asarray(a)
    w_in, w_out, w_gate, w_up, w_down = map(f, (w_in, w_out, w_gate, w_up, w_down))
    sizes = (D, D, D, D, KV_HEADS * DH, KV_HEADS * DH, IH * IDH, IDH, IH, D, D)
    qa, ka, va, qb, kb, vb, qi, ki, wi, ga, gb, end = np.concatenate([[0], np.cumsum(sizes)])
    head = lambda base, h: list(range(base + h * DH, base + (h + 1) * DH))
    chunks = [list(range(ki, wi + IH)), list(range(qi, qi + IH * IDH)), list(range(kb, kb + 512))]
    chunks += [head(qb, h) + head(gb, h) + head(qb, h + 1) + head(gb, h + 1) if dsa
               else head(qa, h) + head(ka, h) + head(va, h) + head(ga, h) for dsa, h in HEAD_CHUNKS]
    stream = np.zeros((DEPTH, UNITS, P, UNIT), np.float32)
    for l in range(DEPTH):
        def put(u, rows):
            k = rows.shape[0] // P
            flat = rows.reshape(k, P, -1).transpose(1, 0, 2).reshape(P, -1)
            stream[l, u, :, :flat.shape[1]] = flat

        put(0, w_in[l][:, chunks[0]])
        for n in range(1, N_CHUNK):
            for i, u in enumerate(chunk_units(n)):
                put(u, w_in[l][i * 512:(i + 1) * 512, chunks[n]])
        for i in range(KT // 2):
            put(OUT_UNIT + i, w_out[l][256 * i:256 * i + 256])
        for j in range(N_FF):
            both = np.concatenate([w_gate[l][:, 256 * j:256 * j + 256], w_up[l][:, 256 * j:256 * j + 256]], axis=1)
            for i in range(2):
                put(up_unit(j) + i, both[i * 512:(i + 1) * 512])
            put(down_unit(j), w_down[l][256 * j:256 * j + 256])
    const = np.zeros((P, N_CONST), np.float32)
    const[:, 0:P] = np.eye(P)
    past = np.arange(P)[None, :] <= np.arange(P)[:, None]
    const[:, P:2 * P] = np.where(past, 0.0, NEG)
    const[:, 3 * P:4 * P] = np.where(past, 0.0, NEG)
    const[:, 4 * P:] = (THETA ** (-np.arange(HALF) / HALF)).astype(np.float32)
    return {
        "x_in": f(x).reshape(TT, P, D).transpose(1, 0, 2),
        "c_in": f(c).reshape(KT, P).T,
        "pos_in": f(positions).reshape(TT, P).T,
        "const_in": const,
        "w_ada": f(w_ada),
        "b_ada": f(b_ada),
        "gains": np.stack([f(g_pre_mix), f(g_post_mix), f(g_pre_ffn), f(g_post_ffn)]),
        "w_stream": stream,
    }


def kernel(**inputs):
    import concourse.bacc as bacc
    from concourse.bass_utils import run_bass_kernel_spmd

    nc = bacc.Bacc("TRN2", target_bir_lowering=False, num_devices=1)
    arrays = {k: np.ascontiguousarray(v) for k, v in laid_out(**inputs).items()}
    args = [nc.dram_tensor(n, arrays[n].shape, mybir.dt.from_np(arrays[n].dtype), kind="ExternalInput").ap() for n in _INS]
    out = nc.dram_tensor("out", (TT, P, D), F32, kind="ExternalOutput").ap()
    hybrid_decoder_trunk(nc, *args, out)
    r = run_bass_kernel_spmd(nc, [arrays], core_ids=[0])
    return r.results[0]["out"].reshape(1, SEQ, D)
```
